# Optimizing a Trainium2 kernel written in Bass

```python
import math
import jax, jax.numpy as jnp
from jax import lax
import numpy as np

D_MODEL = 1024
BATCH = 1
SEQ = 512
DEPTH = 2

N_A = DEPTH // 2
N_B = DEPTH - N_A
POOL_WINDOWS = (2, 4, 8, 16)
N_GROUPS = len(POOL_WINDOWS)
GROUP_DIM = D_MODEL // N_GROUPS
N_HEADS = 8
HEAD_DIM = D_MODEL // (2 * N_HEADS)
V_DIM = 2 * HEAD_DIM
QK_WIDTH = N_HEADS * 2 * HEAD_DIM
V_WIDTH = N_HEADS * V_DIM
D_FF = 4 * D_MODEL
N_BUCKETS = 32
MAX_DISTANCE = 128
Q_BLOCK = 128
EPS = 1e-6

kernel_name = "yoco_pool_diffattn_hybrid"

def _rmsnorm(x, g):
    xf = x.astype(jnp.float32)
    y = xf * lax.rsqrt(jnp.mean(xf * xf, axis=-1, keepdims=True) + EPS)
    return (y * g.astype(jnp.float32)).astype(x.dtype)

def _t5_bucket(rel):
    n = jnp.maximum(rel, 0)
    max_exact = N_BUCKETS // 2
    is_small = n < max_exact
    nf = jnp.maximum(n, 1).astype(jnp.float32)
    large = max_exact + (jnp.log(nf / max_exact) / math.log(MAX_DISTANCE / max_exact)
                         * (N_BUCKETS - max_exact)).astype(jnp.int32)
    large = jnp.minimum(large, N_BUCKETS - 1)
    return jnp.where(is_small, n, large)

def _pool_mixer(h, pool_w, pool_scale):
    b, s, _ = h.shape
    hg = h.reshape(b, s, N_GROUPS, GROUP_DIM).astype(jnp.float32)
    c = jnp.cumsum(hg, axis=1)
    c = jnp.concatenate([jnp.zeros((b, 1, N_GROUPS, GROUP_DIM), jnp.float32), c], axis=1)
    t = jnp.arange(s)
    outs = []
    for g, w in enumerate(POOL_WINDOWS):
        lo = jnp.maximum(t + 1 - w, 0)
        win_sum = c[:, 1:, g] - c[:, lo, g]
        cnt = (t + 1 - lo).astype(jnp.float32)
        outs.append(win_sum / cnt[None, :, None])
    pooled = jnp.stack(outs, axis=2)
    m = (pooled - hg).astype(h.dtype)
    y = jnp.einsum('bsgc,gcd->bsgd', m, pool_w).reshape(b, s, D_MODEL)
    return y * pool_scale

def _mlp(h, w_in, w_out):
    a = jnp.square(jax.nn.relu(h @ w_in))
    return a @ w_out

def _diff_attn(h, k, v, w_q, q_norm, lam_q1, lam_k1, lam_q2, lam_k2, subln, w_o, rel_bias, lambda_init):
    b, s, _ = h.shape
    q = (h @ w_q).reshape(b, s, N_HEADS, 2, HEAD_DIM)
    q = _rmsnorm(q, q_norm) * (HEAD_DIM ** -0.5)
    lam = (jnp.exp(jnp.sum(lam_q1.astype(jnp.float32) * lam_k1.astype(jnp.float32)))
           - jnp.exp(jnp.sum(lam_q2.astype(jnp.float32) * lam_k2.astype(jnp.float32)))
           + lambda_init)
    nb = s // Q_BLOCK
    qb = q.reshape(b, nb, Q_BLOCK, N_HEADS, 2, HEAD_DIM).transpose(1, 0, 2, 3, 4, 5)
    kpos = jnp.arange(s)

    def block(args):
        i, qi = args
        qpos = i * Q_BLOCK + jnp.arange(Q_BLOCK)
        rel = qpos[:, None] - kpos[None, :]
        bias = rel_bias[_t5_bucket(rel)].astype(jnp.float32).transpose(2, 0, 1)
        sc = jnp.einsum('bqhcd,bkhcd->bhcqk', qi, k).astype(jnp.float32)
        sc = sc + bias[None, :, None]
        sc = jnp.where((rel >= 0)[None, None, None], sc, -jnp.inf)
        p = jax.nn.softmax(sc, axis=-1)
        a = p[:, :, 0] - lam * p[:, :, 1]
        return jnp.einsum('bhqk,bkhe->bqhe', a.astype(v.dtype), v)

    o = lax.map(block, (jnp.arange(nb), qb))
    o = o.transpose(1, 0, 2, 3, 4).reshape(b, s, N_HEADS, V_DIM)
    o = _rmsnorm(o, subln) * (1.0 - lambda_init)
    return o.reshape(b, s, V_WIDTH) @ w_o

def setup_inputs(seed: int = 0) -> dict:
    key = jax.random.key(seed)
    ks = jax.random.split(key, 24)
    f = jnp.float32
    nrm = lambda k, shape, sc: jax.random.normal(k, shape, f) * sc
    return {
        "x": nrm(ks[0], (BATCH, SEQ, D_MODEL), 1.0),
        "norm_mix": 1.0 + nrm(ks[1], (DEPTH, D_MODEL), 0.05),
        "norm_mlp": 1.0 + nrm(ks[2], (DEPTH, D_MODEL), 0.05),
        "pool_w": nrm(ks[3], (N_A, N_GROUPS, GROUP_DIM, GROUP_DIM), GROUP_DIM ** -0.5),
        "pool_scale": 1.0 + nrm(ks[4], (N_A, D_MODEL), 0.05),
        "kv_norm": 1.0 + nrm(ks[5], (D_MODEL,), 0.05),
        "w_kv": nrm(ks[6], (D_MODEL, QK_WIDTH + V_WIDTH), D_MODEL ** -0.5),
        "k_norm": 1.0 + nrm(ks[7], (HEAD_DIM,), 0.05),
        "rel_bias": nrm(ks[8], (N_BUCKETS, N_HEADS), 0.5),
        "w_q": nrm(ks[9], (N_B, D_MODEL, QK_WIDTH), D_MODEL ** -0.5),
        "q_norm": 1.0 + nrm(ks[10], (N_B, HEAD_DIM), 0.05),
        "lam_q1": nrm(ks[11], (N_B, HEAD_DIM), 0.1),
        "lam_k1": nrm(ks[12], (N_B, HEAD_DIM), 0.1),
        "lam_q2": nrm(ks[13], (N_B, HEAD_DIM), 0.1),
        "lam_k2": nrm(ks[14], (N_B, HEAD_DIM), 0.1),
        "subln": 1.0 + nrm(ks[15], (N_B, V_DIM), 0.05),
        "w_o": nrm(ks[16], (N_B, V_WIDTH, D_MODEL), V_WIDTH ** -0.5),
        "w_mlp_in": nrm(ks[17], (DEPTH, D_MODEL, D_FF), D_MODEL ** -0.5),
        "w_mlp_out": nrm(ks[18], (DEPTH, D_FF, D_MODEL), D_FF ** -0.5),
    }

def reference(x, norm_mix, norm_mlp, pool_w, pool_scale, kv_norm, w_kv, k_norm, rel_bias,
              w_q, q_norm, lam_q1, lam_k1, lam_q2, lam_k2, subln, w_o, w_mlp_in, w_mlp_out):
    b, s, _ = x.shape
    k_sh = None
    v_sh = None
    for l in range(DEPTH):
        h = _rmsnorm(x, norm_mix[l])
        if l < N_A:
            x = x + _pool_mixer(h, pool_w[l], pool_scale[l])
        else:
            j = l - N_A
            lambda_init = 0.8 - 0.6 * math.exp(-0.3 * l)
            x = x + _diff_attn(h, k_sh, v_sh, w_q[j], q_norm[j], lam_q1[j], lam_k1[j],
                               lam_q2[j], lam_k2[j], subln[j], w_o[j], rel_bias, lambda_init)
        x = x + _mlp(_rmsnorm(x, norm_mlp[l]), w_mlp_in[l], w_mlp_out[l])
        if l == N_A - 1:
            kv = _rmsnorm(x, kv_norm) @ w_kv
            k_sh = _rmsnorm(kv[..., :QK_WIDTH].reshape(b, s, N_HEADS, 2, HEAD_DIM), k_norm)
            v_sh = kv[..., QK_WIDTH:].reshape(b, s, N_HEADS, V_DIM)
    return x


_drawn_inputs = setup_inputs


def setup_inputs(seed=0):
    import zlib

    import numpy as np

    out = dict(_drawn_inputs(seed))
    spreads = {}
    factors = {'k_norm': 5.429,
     'q_norm': 5.02,
     'lam_k1': 3.189,
     'lam_q2': 3.628,
     'lam_k2': 5.322,
     'subln': 3.271}
    for name, (base, spread) in spreads.items():
        noise = np.random.default_rng([zlib.crc32(name.encode()), seed]).standard_normal(out[name].shape)
        drawn = base * np.exp(spread * noise) if base else spread * noise
        out[name] = __import__('jax').numpy.asarray(drawn.astype(out[name].dtype))
    for name, factor in factors.items():
        out[name] = (out[name] * factor).astype(out[name].dtype)
    return out
```

```python
import math

import numpy as np

import concourse.bass as bass
from concourse import mybir
from contextlib import ExitStack

D = 1024
S = 512
P = 128
KC = D // P
TT = S // P
WINDOWS = (2, 4, 8, 16)
G = len(WINDOWS)
GD = D // G
H = 8
HD = D // (2 * H)
FF = 4 * D
NB = 32
MAXD = 128
EPS = 1e-6
LAMBDA_INIT = 0.8 - 0.6 * math.exp(-0.3)
MASKED = -3.0e38
REL = 640
BAND = P + max(WINDOWS) - 1

UNIT = 2048
U_POOL = 0
U_MLP = (1, 53)
U_HEAD = 33
U_WO = 49
UNITS = 85
NF = 2
HALF_CHUNKS = FF // P // 2

C_MIX, C_MLP, C_PSCALE, C_KV, C_QN, C_KN, C_SUB = 0, 16, 32, 40, 48, 49, 50
N_PARAM = 51


def distance_buckets():
    rel = np.arange(S - 1, -1, -1)
    exact = NB // 2
    nf = np.maximum(rel, 1).astype(np.float32)
    large = exact + (np.log(nf / np.float32(exact)) / np.float32(math.log(MAXD / exact)) * np.float32(NB - exact)).astype(np.int32)
    bucket = np.where(rel < exact, rel, np.minimum(large, NB - 1))
    return (np.arange(NB)[:, None] == bucket[None, :]).astype(np.float32)


def build_program(nc, x, norm_mix, norm_mlp, pool_w, pool_scale, kv_norm, w_kv, k_norm, rel_bias,
                  w_q, q_norm, lam_q1, lam_k1, lam_q2, lam_k2, subln, w_o, w_mlp_in, w_mlp_out,
                  bucket_rows, out):
    F32, F32R = mybir.dt.float32, mybir.dt.float32r
    ALU, ACT = mybir.AluOpType, mybir.ActivationFunctionType
    ctx = ExitStack()
    with ctx:
        def sb(name, shape, dt=F32):
            return ctx.enter_context(nc.sbuf_tensor(name, shape, dt))

        def sem(name):
            return ctx.enter_context(nc.semaphore(name))

        xT = sb("xT", [P, KC, S])
        raw = [sb(f"raw{i}", [P, UNIT]) for i in range(2)]
        w_high_buf = [sb(f"w_high{i}", [P, UNIT], F32R) for i in range(2)]
        w_low_buf = [sb(f"w_low{i}", [P, UNIT], F32R) for i in range(2)]
        h_high_buf = sb("h_high_buf", [P, KC, S], F32R)
        h_low_buf = sb("h_low_buf", [P, KC, S], F32R)
        a_high_buf = sb("a_high_buf", [P, HALF_CHUNKS, S], F32R)
        a_low_buf = sb("a_low_buf", [P, HALF_CHUNKS, S], F32R)
        work = sb("work", [P, 11008])
        ident = sb("ident", [P, P])
        params = sb("params", [P, N_PARAM])
        group_ones = sb("group_ones", [P, 2])
        all_ones = sb("all_ones", [P, 2])
        all_halves = sb("all_halves", [P, 2])
        eps = sb("eps", [P, 1])
        qk_gain = sb("qk_gain", [P, 1])
        sub_gain = sb("sub_gain", [P, 1])
        rel_sb = sb("rel_sb", [NB, H])
        tok_ss = sb("tok_ss", [P, TT])
        tok_root = sb("tok_root", [P, TT])
        tok_rstd = sb("tok_rstd", [P, TT])
        norm_root = sb("norm_root", [P, 2 * TT])
        norm_rstd = sb("norm_rstd", [P, TT])
        lam_dots = sb("lam_dots", [P, 2])
        lam_exps = sb("lam_exps", [P, 2])
        neg_lam = sb("neg_lam", [P, 1])
        wait_cell = sb("wait_cell", [1, TT])
        row_max = sb("row_max", [P, 8])
        neg_max = sb("neg_max", [P, 8])
        row_sum = sb("row_sum", [P, 8])
        row_inv = sb("row_inv", [P, 8])
        kq_root_buf = sb("kq_root_buf", [P, 16])
        kq_rstd_buf = sb("kq_rstd_buf", [P, 16])
        o_root_buf = sb("o_root_buf", [P, 2 * TT])
        o_rstd_buf = sb("o_rstd_buf", [P, TT])

        def region(at, n):
            return work[:, at:at + n]

        kf, qf, vf = (region(i * S, S) for i in range(3))
        ksq, qsq, osq = (region((3 + i) * S, S) for i in range(3))
        of = region(3072, S)
        bias_tile = region(3584, S)
        p1_all = region(4096, 1280)
        p2_ring = [region(5376 + i * S, S) for i in range(2)]
        o_all = region(6400, H * S).rearrange("p (h t) -> p h t", h=H)
        rstd_bc = region(10496, S)
        relu_buf = [region(i * S, S) for i in range(2)]
        sq_buf = [region(1024 + i * S, S) for i in range(2)]
        ring = [region(2048 + i * S, S) for i in range(2)]
        ssum = region(3072, S)
        rexp = region(4096, S)
        out_sb = region(6400, TT * D).rearrange("p (i d) -> p i d", i=TT)
        x_tok = region(0, TT * D).rearrange("p (i d) -> p i d", i=TT)
        h_tok = region(4096, TT * D).rearrange("p (i d) -> p i d", i=TT)
        band_first = region(8192, G * BAND).rearrange("p (g n) -> p g n", g=G)
        band_rest = region(8192 + G * BAND, G * BAND).rearrange("p (g n) -> p g n", g=G)
        param_rows = region(9344, P)
        bucket_sb = region(9472, S)
        bias_rows = region(9984, REL)
        lam_sb = region(10624, 4 * HD).rearrange("p (v d) -> p v d", v=4)
        lam_junk = region(10880, HD)

        P1_AT = [0, 128, 384, 768]

        def p1(i):
            return p1_all[:, P1_AT[i]:P1_AT[i] + P * (i + 1)]

        k_hi, k_lo = a_high_buf[:, 8, :], a_low_buf[:, 8, :]
        q_hi, q_lo = [a_high_buf[:, 9 + c, :] for c in range(2)], [a_low_buf[:, 9 + c, :] for c in range(2)]
        v_hi, v_lo = a_high_buf[:, 11, :], a_low_buf[:, 11, :]
        AT_PLACE = [(0, 0), (1, 0), (2, 0), (1, 384)]
        AT_COLS = [512, 512, 256]

        bank = [ctx.enter_context(nc.psum_tensor(f"bank{i}", [P, S], F32)) for i in range(8)]
        O, I = bank[0:4], bank[4:8]

        scratch = nc.dram_tensor("bias_by_distance", (H, P, REL), F32, kind="Internal").ap()

        x_landed = [sem(f"x_landed{i}") for i in range(TT)]
        params_landed = sem("params_landed")
        lam_landed = sem("lam_landed")
        bias_in_landed = sem("bias_in_landed")
        w_landed = [sem(f"w_landed{i}") for i in range(2)]
        bias_stored = sem("bias_stored")
        t_landed = sem("t_landed")
        out_stored = sem("out_stored")
        w_high = sem("w_high")
        w_low = sem("w_low")
        w_used = sem("w_used")
        consts_ready = sem("consts_ready")
        const_steps = sem("const_steps")
        params_turned = sem("params_turned")
        params_ready = sem("params_ready")
        bias_done = sem("bias_done")
        bias_rows_ready = sem("bias_rows_ready")
        tok_sq = sem("tok_sq")
        tok_rooted = sem("tok_rooted")
        tok_inverse = sem("tok_inverse")
        h_tok_ready = sem("h_tok_ready")
        xt_done = sem("xt_done")
        mix_done = sem("mix_done")
        pool_done = sem("pool_done")
        lam_dot = sem("lam_dot")
        lam_exp = sem("lam_exp")
        lam_ready = sem("lam_ready")
        x_ready = sem("x_ready")
        h_high = sem("h_high")
        h_low = sem("h_low")
        norm_sq = sem("norm_sq")
        norm_sum = sem("norm_sum")
        norm_stat = sem("norm_stat")
        norm_rooted = sem("norm_rooted")
        norm_inverse = sem("norm_inverse")
        norm_spread = sem("norm_spread")
        norm_turned = sem("norm_turned")
        rstd_ready = sem("rstd_ready")
        in_first = sem("in_first")
        z_taken = sem("z_taken")
        z_squared = sem("z_squared")
        a_high = sem("a_high")
        a_low = sem("a_low")
        out_done = sem("out_done")
        k_proj = sem("k_proj")
        kf_ready = sem("kf_ready")
        qf_ready = sem("qf_ready")
        vf_ready = sem("vf_ready")
        kq_sq = sem("kq_sq")
        kq_stat = sem("kq_stat")
        kq_rooted = sem("kq_rooted")
        kq_inverse = sem("kq_inverse")
        k_spread = sem("k_spread")
        q_spread = sem("q_spread")
        k_turned = sem("k_turned")
        q_turned = sem("q_turned")
        kn_ready = sem("kn_ready")
        qn_ready = sem("qn_ready")
        kq_high = sem("kq_high")
        kq_low = sem("kq_low")
        v_turned = sem("v_turned")
        v_high = sem("v_high")
        v_low = sem("v_low")
        s_done = sem("s_done")
        s_taken = sem("s_taken")
        max_ready = sem("max_ready")
        exp_done = sem("exp_done")
        inv_ready = sem("inv_ready")
        second_scaled = sem("second_scaled")
        a_ready = sem("a_ready")
        at_done = sem("at_done")
        at_high = sem("at_high")
        at_low = sem("at_low")
        pv_done = sem("pv_done")
        o_copied = sem("o_copied")
        o_stat = sem("o_stat")
        o_rooted = sem("o_rooted")
        o_inverse = sem("o_inverse")
        o_spread = sem("o_spread")
        o_turned = sem("o_turned")
        o_ready = sem("o_ready")
        y_turned = sem("y_turned")
        y_copied = [sem(f"y_copied{i}") for i in range(2)]

        BAND_STEPS = 8 + sum(8 + w - 1 for w in WINDOWS)
        X_POOL, X_MLP, X_WO = 8, (16, 40), 32
        H_POOL, H_MLP, H_K, H_Q, H_O = 0, (8, 40), 16, 24, 32
        OUT_MLP, OUT_WO = (0, 18), 12
        NORM_MLP, NORM_KV = (0, 2), 1

        def landed(u0, i=0):
            count = 16 * (u0 // 2 + 1)
            if u0 % 2 and u0 >= U_WO:
                count += 16 * H + 16
            return count + 16 * i

        def head_landed(n):
            return 16 * (U_HEAD // 2) + 32 * (n + 1)

        pool_v = pool_w[0].rearrange("g (k p) n -> p g k n", p=P)
        wk_v = w_kv.rearrange("(k p) n -> p k n", p=P)
        wq_v = w_q[0].rearrange("(k p) n -> p k n", p=P)
        wo_v = w_o[0].rearrange("(k p) n -> p k n", p=P)
        win_v = [w_mlp_in[l].rearrange("(k p) n -> p k n", p=P) for l in range(2)]
        wout_v = [w_mlp_out[l].rearrange("(k p) n -> p k n", p=P) for l in range(2)]

        def tile3(t, k):
            return t[:, :].rearrange("p (k n) -> p k n", k=k)

        block = ctx.enter_context(nc.Block())

        @block.sync
        def _(sp):
            for i in range(TT):
                sp.dma_start(x_tok[:, i, :], x[0, i * P:(i + 1) * P, :]).then_inc(x_landed[i], 16)
            sp.dma_start(raw[0][:, :].rearrange("p (g k n) -> p g k n", g=G, k=GD // P), pool_v).then_inc(w_landed[0], 16)

            def slot_free(u):
                sp.wait_ge(w_low, u - 1)

            def load_in(l, u, s, column):
                slot_free(u)
                sp.dma_start(tile3(raw[s], KC), win_v[l][:, :, bass.ds(column, 2 * P)]).then_inc(w_landed[s], 16)

            def load_mlp(l):
                for half in range(2):
                    u0 = U_MLP[l] + 16 * half
                    if l == 0 and half == 0:
                        sp.dma_start(tile3(raw[1], KC), win_v[l][:, :, 0:2 * P]).then_inc(w_landed[1], 16)
                        load_in(l, u0 + 1, 0, 2 * P)
                        first = 1
                    else:
                        first = 0
                    with sp.Fori(first, 4) as i:
                        for j in range(2):
                            load_in(l, u0 + 2 * i + j, (u0 + j) % 2, half * 2048 + 512 * i + 256 * j)
                    for f in range(NF):
                        with sp.Fori(0, 2) as r:
                            for j in range(2):
                                u = u0 + 8 + 4 * f + j
                                slot_free(u + 2 * r)
                                sp.dma_start(tile3(raw[u % 2], 4),
                                             wout_v[l][:, bass.ds(half * HALF_CHUNKS + 8 * r + 4 * j, 4), f * S:(f + 1) * S])\
                                  .then_inc(w_landed[u % 2], 16)

            load_mlp(0)
            with sp.Fori(0, H) as n:
                slot_free(U_HEAD + 2 * n)
                sp.dma_start(tile3(raw[1][:, 0:1024], KC), wk_v[:, :, bass.ds(n * P, P)]).then_inc(w_landed[1], 16)
                sp.dma_start(tile3(raw[1][:, 1024:2048], KC), wq_v[:, :, bass.ds(n * P, P)]).then_inc(w_landed[1], 16)
                slot_free(U_HEAD + 1 + 2 * n)
                sp.dma_start(tile3(raw[0][:, 0:1024], KC), wk_v[:, :, bass.ds(D + n * P, P)]).then_inc(w_landed[0], 16)
            for f in range(NF):
                for q in range(2):
                    u = U_WO + 2 * f + q
                    slot_free(u)
                    if u == U_WO:
                        for b in range(2):
                            sp.dma_start(tile3(raw[1][:, b * 1024:(b + 1) * 1024], 2),
                                         wo_v[:, 2 * b:2 * b + 2, 0:S]).then_inc(w_landed[1], 16)
                    else:
                        sp.dma_start(tile3(raw[u % 2], 4), wo_v[:, 4 * q:4 * q + 4, f * S:(f + 1) * S])\
                          .then_inc(w_landed[u % 2], 16)
            load_mlp(1)
            for f in range(NF):
                for i in range(TT):
                    sp.wait_ge(y_copied[i % 2], 2 * f + i // 2 + 1)
                    sp.dma_start(out[0, i * P:(i + 1) * P, f * S:(f + 1) * S], out_sb[:, i, f * S:(f + 1) * S])\
                      .then_inc(out_stored, 16)
            sp.wait_ge(out_stored, 16 * NF * TT)

        @block.gpsimd
        def _(pool):
            steps = [0]

            def done(instruction):
                steps[0] += 1
                instruction.then_inc(const_steps, 1)
                pool.wait_ge(const_steps, steps[0])

            done(pool.memset(ident[:, :], 0.0))
            done(pool.affine_select(out=ident[:, :], in_=ident[:, :], compare_op=ALU.not_equal, fill=1.0, base=0,
                                    pattern=[[-1, P]], channel_multiplier=1))
            done(pool.memset(all_ones[:, :], 1.0))
            done(pool.memset(a_high_buf[:, 0, :].bitcast(F32), 0.0))
            done(pool.memset(all_halves[:, :], 0.5))
            done(pool.memset(group_ones[:, :], 0.0))
            done(pool.memset(group_ones[0:HD, 0:1], 1.0))
            done(pool.memset(group_ones[HD:P, 1:2], 1.0))
            pool.memset(eps[:, :], EPS).then_inc(consts_ready, 1)
            for g, w in enumerate(WINDOWS):
                for b in (band_first, band_rest):
                    done(pool.memset(b[:, g, :], 1.0 / w))
                for n in range(w - 1):
                    done(pool.memset(band_first[:, g, n:n + 1], 1.0 / (n + 1)))
                for b in (band_first, band_rest):
                    done(pool.affine_select(out=b[:, g, :], in_=b[:, g, :], compare_op=ALU.is_ge, fill=0.0, base=0,
                                            pattern=[[1, BAND]], channel_multiplier=-1))
                    done(pool.affine_select(out=b[:, g, :], in_=b[:, g, :], compare_op=ALU.is_ge, fill=0.0, base=w - 1,
                                            pattern=[[-1, BAND]], channel_multiplier=1))
                    done(pool.tensor_tensor(b[:, g, 0:P], b[:, g, 0:P], ident[:, :], ALU.subtract))
            pool.wait_ge(bias_rows_ready, 2)
            pool.dma_start(scratch, bias_rows[0:H, :].unsqueeze(1).to_broadcast([H, P, REL])).then_inc(bias_stored, 16)
            pool.wait_ge(bias_stored, 16)
            pool.wait_ge(w_used, U_HEAD)
            for q in (q_hi, q_lo):
                done(pool.memset(q[0][HD:P, :].bitcast(F32), 0.0))
                done(pool.memset(q[1][0:HD, :].bitcast(F32), 0.0))
            for h in range(H):
                if h:
                    pool.wait_ge(s_taken, 8 * h)
                pool.dma_start(bias_tile, bass.AP(tensor=scratch.tensor, offset=h * P * REL + P - 1, ap=[[REL - 1, P], [1, S]]))\
                    .then_inc(t_landed, 16)

        @block.scalar
        def _(act):
            def split_high(u, s, landed_count, cols=UNIT):
                act.wait_ge(w_landed[s], landed_count)
                if not isinstance(u, int) or u >= 2:
                    act.wait_ge(w_used, u - 1)
                act.activation(w_high_buf[s][:, 0:cols], raw[s][:, 0:cols], ACT.Copy).then_inc(w_high, 1)

            def input_high(dst, src, gain):
                act.activation(dst, src, ACT.Copy, scale=gain).then_inc(h_high, 1)

            def norm_squares(n):
                for c in range(KC):
                    if c >= 3:
                        act.wait_ge(norm_sum, 7 * n + c - 2)
                    act.activation(ssum if c == 0 else ring[(c - 1) % 2], xT[:, c, :], ACT.Square).then_inc(norm_sq, 1)

            def norm_root_step(n):
                act.wait_ge(norm_stat, n + 1)
                act.activation(norm_root[:, :], O[3][:, 0:2 * TT], ACT.Sqrt, scale=1.0 / D, bias=eps[:, 0:1])\
                   .then_inc(norm_rooted, 1)

            def prep_x(h_base, x_base, dst, gain):
                for c in range(KC):
                    act.wait_ge(x_ready, x_base + c + 1)
                    input_high(dst[:, c, :], xT[:, c, :], params[:, gain + c:gain + c + 1])

            def hidden(c, k):
                for j in range(2):
                    cc, kk = c + j, k + j
                    s = j
                    act.wait_ge(z_taken, cc + 1)
                    if not isinstance(cc, int) or cc >= 2:
                        act.wait_ge(a_low, cc - 1)
                    act.activation(sq_buf[s], relu_buf[s], ACT.Square).then_inc(z_squared, 1)
                    act.wait_ge(z_squared, cc + 1)
                    act.activation(a_high_buf[:, bass.ds(kk, 1), :] if not isinstance(kk, int) else a_high_buf[:, kk, :],
                                   sq_buf[s], ACT.Copy).then_inc(a_high, 1)

            def mlp(l):
                for half in range(2):
                    u0, c0 = U_MLP[l] + 16 * half, 32 * l + 16 * half
                    first = 0
                    if half == 0:
                        split_high(u0 + 1, (u0 + 1) % 2, landed(u0 + 1))
                        norm_squares(NORM_MLP[l])
                        norm_root_step(NORM_MLP[l])
                        hidden(c0, 0)
                        split_high(u0 + 2, u0 % 2, landed(u0 + 2))
                        hidden(c0 + 2, 2)
                        first = 1
                    with act.Fori(first, 4) as i:
                        for j in range(2):
                            split_high(u0 + 1 + j + 2 * i, (u0 + 1 + j) % 2, landed(u0 + 1 + j, i))
                            hidden(c0 + 2 * j + 4 * i, 2 * j + 4 * i)
                    for f in range(NF):
                        u = u0 + 8 + 4 * f + 1
                        if half == 1 and f == 1:
                            for q in range(3):
                                split_high(u + q, (u + q) % 2, landed(u + q))
                            if l == 0:
                                split_high(U_HEAD, 1, head_landed(0))
                        else:
                            with act.Fori(0, 2) as r:
                                for j in range(2):
                                    split_high(u + j + 2 * r, (u + j) % 2, landed(u + j, r))

            act.dma_start(param_rows[0:16, :], norm_mix.rearrange("l (k p) -> (l k) p", p=P)).then_inc(params_landed, 16)
            act.dma_start(param_rows[16:32, :], norm_mlp.rearrange("l (k p) -> (l k) p", p=P)).then_inc(params_landed, 16)
            act.dma_start(param_rows[32:40, :], pool_scale[0].rearrange("(k p) -> k p", p=P)).then_inc(params_landed, 16)
            act.dma_start(param_rows[40:48, :], kv_norm.rearrange("(k p) -> k p", p=P)).then_inc(params_landed, 16)
            for c in range(2):
                act.dma_start(param_rows[48:49, c * HD:(c + 1) * HD], q_norm[0:1, :]).then_inc(params_landed, 16)
                act.dma_start(param_rows[49:50, c * HD:(c + 1) * HD], k_norm.rearrange("(a d) -> a d", a=1)).then_inc(params_landed, 16)
            act.dma_start(param_rows[50:51, :], subln[0:1, :]).then_inc(params_landed, 16)
            act.dma_start(bucket_sb[0:NB, :], bucket_rows).then_inc(bias_in_landed, 16)
            act.dma_start(rel_sb[:, :], rel_bias).then_inc(bias_in_landed, 16)
            for v, lam in enumerate((lam_q1, lam_k1, lam_q2, lam_k2)):
                act.dma_start(lam_sb[:, v, :], lam[0:1, :].to_broadcast([P, HD])).then_inc(lam_landed, 16)
            for i in range(TT):
                act.wait_ge(x_landed[i], 16)
                act.activation(h_tok[:, i, :], x_tok[:, i, :], ACT.Square, accum_out=tok_ss[:, i:i + 1]).then_inc(tok_sq, 1)
            act.wait_ge(tok_sq, TT)
            act.wait_ge(consts_ready, 1)
            act.activation(tok_root[:, :], tok_ss[:, :], ACT.Sqrt, scale=1.0 / D, bias=eps[:, 0:1]).then_inc(tok_rooted, 1)
            split_high(0, 0, 16)
            act.wait_ge(params_ready, 1)
            for c in range(KC):
                act.wait_ge(mix_done, c + 1)
                input_high(h_high_buf[:, c, :], I[c % 4][:, :], params[:, C_MIX + c:C_MIX + c + 1])
            split_high(1, 1, 16)
            act.wait_ge(lam_dot, 2)
            act.activation(lam_exps[:, :], lam_dots[:, :], ACT.Exp).then_inc(lam_exp, 1)
            act.wait_ge(bias_done, 1)
            act.activation(bias_rows[0:H, 0:S], O[0][0:H, :], ACT.Copy).then_inc(bias_rows_ready, 1)
            act.wait_ge(w_used, 1)
            prep_x(H_MLP[0], X_POOL, h_high_buf, C_MLP)
            mlp(0)

            def project(n):
                act.wait_ge(kf_ready, n + 1)
                act.activation(ksq, kf, ACT.Square).then_inc(kq_sq, 1)

            def project_q(n):
                act.wait_ge(qf_ready, n + 1)
                act.activation(qsq, qf, ACT.Square).then_inc(kq_sq, 1)

            def kq_roots(n):
                act.wait_ge(kq_stat, n + 1)
                act.activation(kq_root_buf[:, :], I[3][:, 0:16], ACT.Sqrt, scale=1.0 / HD, bias=eps[:, 0:1]).then_inc(kq_rooted, 1)

            def kq_highs(n):
                act.wait_ge(kn_ready, n + 1)
                act.activation(k_hi, kf, ACT.Copy).then_inc(kq_high, 1)
                act.wait_ge(qn_ready, n + 1)
                for c in range(2):
                    r = slice(c * HD, (c + 1) * HD)
                    act.activation(q_hi[c][r, :], qf[r, :], ACT.Copy, scale=qk_gain[r, 0:1]).then_inc(kq_high, 1)

            def v_highs(n):
                act.wait_ge(v_turned, n + 1)
                act.activation(v_hi, I[2][:, :], ACT.Copy).then_inc(v_high, 1)

            def exps(h):
                for i in range(TT):
                    act.wait_ge(max_ready, 4 * h + i + 1)
                    for c in range(2):
                        t = p1(i) if c == 0 else p2_ring[i % 2][:, 0:P * (i + 1)]
                        act.activation(t, t, ACT.Exp, bias=neg_max[:, 2 * i + c:2 * i + c + 1],
                                       accum_out=row_sum[:, 2 * i + c:2 * i + c + 1]).then_inc(exp_done, 1)

            def at_highs(h):
                act.wait_ge(at_done, h + 1)
                for b in range(3):
                    act.activation(a_high_buf[:, 12 + b, 0:AT_COLS[b]], O[b][:, 0:AT_COLS[b]], ACT.Copy).then_inc(at_high, 1)

            def o_roots(m, b):
                act.wait_ge(o_stat, m + 1)
                act.activation(o_root_buf[:, :], b[:, 16:16 + 2 * TT], ACT.Sqrt, scale=1.0 / HD, bias=eps[:, 0:1]).then_inc(o_rooted, 1)

            def o_copies(h):
                act.wait_ge(pv_done, h + 1)
                act.activation(of, O[3][:, :], ACT.Copy).then_inc(o_copied, 1)
                act.activation(osq, O[3][:, :], ACT.Square).then_inc(o_copied, 1)

            def o_high(k):
                act.wait_ge(o_ready, k + 1)
                input_high(h_high_buf[:, k, :], o_all[:, k, :], sub_gain[:, 0:1])

            prep_x(H_K, X_MLP[0] + 8, h_high_buf, C_KV)
            prep_x(H_Q, X_MLP[0] + 8, a_high_buf, C_MIX + KC)
            norm_squares(NORM_KV)
            norm_root_step(NORM_KV)
            split_high(U_HEAD + 1, 0, landed(U_HEAD + 1), 1024)
            project(0)
            project_q(0)
            kq_roots(0)
            split_high(U_HEAD + 2, 1, head_landed(1))
            kq_highs(0)
            v_highs(0)

            def head(h, first):
                exps(h)
                split_high(U_HEAD + 3 + 2 * h, 0, landed(U_HEAD + 3, h), 1024)
                project(h + 1)
                project_q(h + 1)
                at_highs(h)
                kq_roots(h + 1)
                if not first:
                    o_roots(h - 1, I[3])
                split_high(U_HEAD + 4 + 2 * h, 1, head_landed(h + 2))
                kq_highs(h + 1)
                o_copies(h)
                v_highs(h + 1)

            head(0, True)
            with act.Fori(1, H - 1) as h:
                head(h, False)
            exps(H - 1)
            split_high(U_WO + 1, 0, landed(U_WO + 1))
            o_roots(H - 2, I[3])
            act.wait_ge(w_used, U_WO)
            for k in range(4):
                o_high(k)
            at_highs(H - 1)
            for k in range(4, H - 1):
                o_high(k)
            o_copies(H - 1)
            o_roots(H - 1, O[0])
            split_high(U_WO + 2, 1, landed(U_WO + 2))
            o_high(H - 1)
            split_high(U_WO + 3, 0, landed(U_WO + 3))
            split_high(U_WO + 4, 1, landed(U_WO + 4))
            act.wait_ge(w_used, U_MLP[1])
            prep_x(H_MLP[1], X_WO, h_high_buf, C_MLP + KC)

            def copy_result(f):
                for i in (0, 2):
                    act.wait_ge(y_turned, 4 * f + i + 1)
                    act.activation(out_sb[:, i, f * S:(f + 1) * S], I[i][:, :], ACT.Copy).then_inc(y_copied[0], 1)

            mlp(1)
            for f in range(NF):
                copy_result(f)

        @block.vector
        def _(dve):
            def f32(t):
                return t.bitcast(F32)

            def split_low(u, s, cols=UNIT):
                dve.wait_ge(w_high, u + 1)
                dve.tensor_tensor(w_low_buf[s][:, 0:cols], raw[s][:, 0:cols], f32(w_high_buf[s][:, 0:cols]), ALU.subtract)\
                   .then_inc(w_low, 1)

            def input_low(dst, src, gain, high):
                dve.scalar_tensor_tensor(dst, src, gain, f32(high), ALU.mult, ALU.subtract).then_inc(h_low, 1)

            def prep_x(h_base, hi, lo, gain):
                for c in range(KC):
                    dve.wait_ge(h_high, h_base + c + 1)
                    input_low(lo[:, c, :], xT[:, c, :], params[:, gain + c:gain + c + 1], hi[:, c, :])

            def norm_sums(n):
                for c in range(1, KC):
                    dve.wait_ge(norm_sq, 8 * n + c + 1)
                    if c > 1:
                        dve.wait_ge(norm_sum, 7 * n + c - 1)
                    dve.tensor_tensor(ssum, ssum, ring[(c - 1) % 2], ALU.add).then_inc(norm_sum, 1)

            def norm_finish(n):
                dve.wait_ge(norm_rooted, n + 1)
                dve.reciprocal(norm_rstd[:, :], norm_root[:, :].rearrange("p (i b) -> p i b", b=2)[:, :, 0]).then_inc(norm_inverse, 1)
                dve.wait_ge(norm_inverse, n + 1)
                dve.tensor_copy(rexp.rearrange("p (i n) -> p i n", i=TT), norm_rstd[:, :].unsqueeze(2).to_broadcast([P, TT, P]))\
                   .then_inc(norm_spread, 1)
                dve.wait_ge(norm_turned, n + 1)
                dve.tensor_copy(rstd_bc, O[2][:, :]).then_inc(rstd_ready, 1)
                dve.wait_ge(rstd_ready, n + 1)

            def hidden(u, n_in, c, k, odd):
                for j in range(2):
                    cc, kk = c + j, k + j
                    if j == 0:
                        dve.wait_ge(in_first, n_in + 1)
                    else:
                        dve.wait_ge(w_used, u + 1)
                    if not isinstance(cc, int) or cc >= 2:
                        dve.wait_ge(z_squared, cc - 1)
                    dve.scalar_tensor_tensor(relu_buf[j], I[2 * odd + j][:, :], 0.0, rstd_bc, ALU.max, ALU.mult)\
                       .then_inc(z_taken, 1)
                    dve.wait_ge(a_high, cc + 1)
                    hi = a_high_buf[:, kk, :] if isinstance(kk, int) else a_high_buf[:, bass.ds(kk, 1), :]
                    lo = a_low_buf[:, kk, :] if isinstance(kk, int) else a_low_buf[:, bass.ds(kk, 1), :]
                    dve.tensor_tensor(lo, sq_buf[j], f32(hi), ALU.subtract).then_inc(a_low, 1)

            def mlp(l):
                for half in range(2):
                    u0, c0 = U_MLP[l] + 16 * half, 32 * l + 16 * half
                    n0 = 16 * l + 8 * half
                    first = 0
                    if half == 0:
                        split_low(u0 + 1, (u0 + 1) % 2)
                        norm_sums(NORM_MLP[l])
                        norm_finish(NORM_MLP[l])
                        hidden(u0, n0, c0, 0, 0)
                        split_low(u0 + 2, u0 % 2)
                        hidden(u0 + 1, n0 + 1, c0 + 2, 2, 1)
                        first = 1
                    with dve.Fori(first, 4) as i:
                        for j in range(2):
                            split_low(u0 + 1 + j + 2 * i, (u0 + 1 + j) % 2)
                            hidden(u0 + j + 2 * i, n0 + j + 2 * i, c0 + 2 * j + 4 * i, 2 * j + 4 * i, j)
                    for f in range(NF):
                        last_phase = l == 1 and half == 1 and f == 1
                        if last_phase:
                            for q in range(3):
                                split_low(u0 + 13 + q, (u0 + 13 + q) % 2)
                            copy_result(0)
                        else:
                            with dve.Fori(0, 2) as r:
                                for j in range(2):
                                    u = u0 + 8 + 4 * f + 1 + j
                                    split_low(u + 2 * r, u % 2)
                        for m in range(4):
                            if m < 3:
                                dve.wait_ge(out_done, OUT_MLP[l] + 6 * half + 3 * f + m + 1)
                            else:
                                dve.wait_ge(w_used, u0 + 8 + 4 * f + 4)
                            dve.tensor_tensor(xT[:, 4 * f + m, :], xT[:, 4 * f + m, :], O[m][:, :], ALU.add).then_inc(x_ready, 1)

            def copy_result(f):
                for i in (1, 3):
                    dve.wait_ge(y_turned, 4 * f + i + 1)
                    dve.tensor_copy(out_sb[:, i, f * S:(f + 1) * S], I[i][:, :]).then_inc(y_copied[1], 1)

            dve.memset(bias_rows[0:H, S:REL], MASKED).then_inc(bias_rows_ready, 1)
            dve.wait_ge(lam_landed, 64)
            for b in range(2):
                dve.tensor_tensor_reduce(out=lam_junk, in0=lam_sb[:, 2 * b, :], in1=lam_sb[:, 2 * b + 1, :], scale=1.0, scalar=0.0,
                                         op0=ALU.mult, op1=ALU.add, accum_out=lam_dots[:, b:b + 1]).then_inc(lam_dot, 1)
                dve.wait_ge(lam_dot, b + 1)
            dve.wait_ge(params_turned, 1)
            dve.tensor_copy(params[:, :], I[3][:, 0:N_PARAM]).then_inc(params_ready, 1)
            dve.wait_ge(params_ready, 1)
            dve.tensor_scalar(qk_gain[:, :], params[:, C_QN:C_QN + 1], params[:, C_KN:C_KN + 1], HD ** -0.5, ALU.mult, ALU.mult)
            dve.tensor_scalar(sub_gain[:, :], params[:, C_SUB:C_SUB + 1], 1.0 - LAMBDA_INIT, None, ALU.mult).then_inc(params_ready, 1)
            dve.wait_ge(tok_rooted, 1)
            dve.reciprocal(tok_rstd[:, :], tok_root[:, :]).then_inc(tok_inverse, 1)
            dve.wait_ge(tok_inverse, 1)
            for i in range(TT):
                dve.tensor_scalar(h_tok[:, i, :], x_tok[:, i, :], tok_rstd[:, i:i + 1], None, ALU.mult).then_inc(h_tok_ready, 1)
            for c in range(KC):
                dve.wait_ge(xt_done, c + 1)
                dve.tensor_copy(xT[:, c, :], O[c % 4][:, :]).then_inc(x_ready, 1)
            split_low(0, 0)
            for c in range(KC):
                dve.wait_ge(h_high, H_POOL + c + 1)
                input_low(h_low_buf[:, c, :], I[c % 4][:, :], params[:, C_MIX + c:C_MIX + c + 1], h_high_buf[:, c, :])
            split_low(1, 1)
            dve.wait_ge(lam_exp, 1)
            dve.tensor_scalar(neg_lam[:, :], lam_exps[:, 1:2], lam_exps[:, 0:1], -LAMBDA_INIT, ALU.subtract, ALU.add).then_inc(lam_ready, 1)
            for c in range(KC):
                if c < KC - 1:
                    dve.wait_ge(pool_done, c + 1)
                else:
                    dve.wait_ge(w_used, 1)
                dve.scalar_tensor_tensor(xT[:, c, :], I[c % 4][:, :], params[:, C_PSCALE + c:C_PSCALE + c + 1], xT[:, c, :],
                                         ALU.mult, ALU.add).then_inc(x_ready, 1)
            dve.wait_ge(x_ready, X_MLP[0])
            dve.wait_ge(bias_stored, 16)
            prep_x(H_MLP[0], h_high_buf, h_low_buf, C_MLP)
            mlp(0)

            def take_k(n):
                dve.wait_ge(k_proj, n + 1)
                dve.tensor_tensor(kf, I[0][:, :], rstd_bc, ALU.mult).then_inc(kf_ready, 1)

            def take_q(n):
                dve.wait_ge(w_used, U_HEAD + 1 + 2 * n)
                dve.tensor_tensor(qf, I[1][:, :], rstd_bc, ALU.mult).then_inc(qf_ready, 1)

            def take_v(n):
                dve.wait_ge(w_used, U_HEAD + 2 + 2 * n)
                dve.tensor_tensor(vf, I[2][:, :], rstd_bc, ALU.mult).then_inc(vf_ready, 1)

            def kq_inverses(n):
                dve.wait_ge(kq_rooted, n + 1)
                dve.reciprocal(kq_rstd_buf[:, :], kq_root_buf[:, :]).then_inc(kq_inverse, 1)
                dve.wait_ge(kq_inverse, n + 1)
                for b, (dst, s) in enumerate(((ksq, k_spread), (qsq, q_spread))):
                    dve.tensor_copy(dst.rearrange("p (g d) -> p g d", d=HD),
                                    kq_rstd_buf[:, 8 * b:8 * b + 8].unsqueeze(2).to_broadcast([P, 8, HD])).then_inc(s, 1)

            def kq_norms(n):
                dve.wait_ge(k_turned, n + 1)
                dve.tensor_tensor(kf, kf, I[0][:, :], ALU.mult).then_inc(kn_ready, 1)
                dve.wait_ge(q_turned, n + 1)
                dve.tensor_tensor(qf, qf, I[1][:, :], ALU.mult).then_inc(qn_ready, 1)

            def kq_lows(n):
                dve.wait_ge(kq_high, 3 * n + 1)
                dve.tensor_tensor(k_lo, kf, f32(k_hi), ALU.subtract).then_inc(kq_low, 1)
                for c in range(2):
                    r = slice(c * HD, (c + 1) * HD)
                    dve.wait_ge(kq_high, 3 * n + 2 + c)
                    dve.scalar_tensor_tensor(q_lo[c][r, :], qf[r, :], qk_gain[r, 0:1], f32(q_hi[c][r, :]),
                                             ALU.mult, ALU.subtract).then_inc(kq_low, 1)

            def v_lows(n):
                dve.wait_ge(v_high, n + 1)
                dve.tensor_tensor(v_lo, I[2][:, :], f32(v_hi), ALU.subtract).then_inc(v_low, 1)

            def scores(h, i):
                if i >= 2:
                    dve.wait_ge(a_ready, 4 * h + i - 1)
                dve.wait_ge(s_done, 8 * h + 2 * i + 2)
                dve.memset(wait_cell[0:1, i:i + 1], 0.0)
                for c in range(2):
                    j = 2 * i + c
                    t = p1(i) if c == 0 else p2_ring[i % 2][:, 0:P * (i + 1)]
                    dve.tensor_tensor_reduce(out=t, in0=O[j % 4][:, 0:P * (i + 1)], in1=bias_tile[:, P * (3 - i):S],
                                             scale=1.0, scalar=MASKED, op0=ALU.add, op1=ALU.max,
                                             accum_out=row_max[:, j:j + 1]).then_inc(s_taken, 1)
                dve.wait_ge(s_taken, 8 * h + 2 * i + 2)
                dve.tensor_scalar(neg_max[:, 2 * i:2 * i + 2], row_max[:, 2 * i:2 * i + 2], -1.0, None, ALU.mult).then_inc(max_ready, 1)

            def combine(h, i):
                t2 = p2_ring[i % 2][:, 0:P * (i + 1)]
                dve.wait_ge(exp_done, 8 * h + 2 * i + 2)
                dve.reciprocal(row_inv[:, 2 * i:2 * i + 2], row_sum[:, 2 * i:2 * i + 2]).then_inc(inv_ready, 1)
                dve.wait_ge(inv_ready, 4 * h + i + 1)
                dve.tensor_scalar(t2, t2, row_inv[:, 2 * i + 1:2 * i + 2], neg_lam[:, 0:1], ALU.mult, ALU.mult).then_inc(second_scaled, 1)
                dve.wait_ge(second_scaled, 4 * h + i + 1)
                dve.scalar_tensor_tensor(p1(i), p1(i), row_inv[:, 2 * i:2 * i + 1], t2, ALU.mult, ALU.add).then_inc(a_ready, 1)

            def at_lows(h):
                for b in range(3):
                    dve.wait_ge(at_high, 3 * h + b + 1)
                    dve.tensor_tensor(a_low_buf[:, 12 + b, 0:AT_COLS[b]], O[b][:, 0:AT_COLS[b]],
                                      f32(a_high_buf[:, 12 + b, 0:AT_COLS[b]]), ALU.subtract).then_inc(at_low, 1)

            def o_inverses(m):
                dve.wait_ge(o_rooted, m + 1)
                dve.reciprocal(o_rstd_buf[:, :], o_root_buf[:, :].rearrange("p (i b) -> p i b", b=2)[:, :, 0]).then_inc(o_inverse, 1)
                dve.wait_ge(o_inverse, m + 1)
                dve.tensor_copy(osq.rearrange("p (i n) -> p i n", i=TT), o_rstd_buf[:, :].unsqueeze(2).to_broadcast([P, TT, P]))\
                   .then_inc(o_spread, 1)

            def o_norm(m, b):
                dve.wait_ge(o_turned, m + 1)
                dst = o_all[:, m, :] if isinstance(m, int) else o_all[:, bass.ds(m, 1), :]
                dve.tensor_tensor(dst, of, b[:, :], ALU.mult).then_inc(o_ready, 1)

            def o_low(k):
                dve.wait_ge(h_high, H_O + k + 1)
                input_low(h_low_buf[:, k, :], o_all[:, k, :], sub_gain[:, 0:1], h_high_buf[:, k, :])

            dve.wait_ge(x_ready, X_MLP[0] + 16)
            prep_x(H_K, h_high_buf, h_low_buf, C_KV)
            prep_x(H_Q, a_high_buf, a_low_buf, C_MIX + KC)
            norm_sums(NORM_KV)
            norm_finish(NORM_KV)
            take_k(0)
            split_low(U_HEAD + 1, 0, 1024)
            take_q(0)
            kq_inverses(0)
            split_low(U_HEAD + 2, 1)
            take_v(0)
            kq_norms(0)
            kq_lows(0)
            v_lows(0)
            dve.wait_ge(lam_ready, 1)

            def head(h, first):
                dve.wait_ge(t_landed, 16 * h + 16)
                scores(h, 0)
                scores(h, 1)
                combine(h, 0)
                scores(h, 2)
                combine(h, 1)
                scores(h, 3)
                combine(h, 2)
                combine(h, 3)
                take_k(h + 1)
                split_low(U_HEAD + 3 + 2 * h, 0, 1024)
                take_q(h + 1)
                at_lows(h)
                kq_inverses(h + 1)
                if not first:
                    o_inverses(h - 1)
                split_low(U_HEAD + 4 + 2 * h, 1)
                take_v(h + 1)
                if not first:
                    o_norm(h - 1, O[3])
                kq_norms(h + 1)
                kq_lows(h + 1)
                v_lows(h + 1)

            head(0, True)
            with dve.Fori(1, H - 1) as h:
                head(h, False)
            last = H - 1
            dve.wait_ge(t_landed, 16 * last + 16)
            scores(last, 0)
            scores(last, 1)
            combine(last, 0)
            scores(last, 2)
            combine(last, 1)
            scores(last, 3)
            combine(last, 2)
            combine(last, 3)
            split_low(U_WO + 1, 0)
            o_inverses(last - 1)
            for k in range(4):
                o_low(k)
            o_norm(last - 1, O[3])
            at_lows(last)
            for k in range(4, last):
                o_low(k)
            o_inverses(last)
            split_low(U_WO + 2, 1)
            o_norm(last, O[1])
            o_low(last)
            split_low(U_WO + 3, 0)
            for f in range(NF):
                acc = I if f == 0 else O
                if f == 1:
                    split_low(U_WO + 4, 1)
                for m in range(4):
                    if m < 3:
                        dve.wait_ge(out_done, OUT_WO + 3 * f + m + 1)
                    else:
                        dve.wait_ge(w_used, U_WO + 2 * f + 2)
                    dve.tensor_tensor(xT[:, 4 * f + m, :], xT[:, 4 * f + m, :], acc[m][:, :], ALU.add).then_inc(x_ready, 1)
            dve.wait_ge(x_ready, X_MLP[1])
            prep_x(H_MLP[1], h_high_buf, h_low_buf, C_MLP + KC)
            mlp(1)
            copy_result(1)

        @block.tensor
        def _(pe):
            def product(acc, w_hi, w_lo, m_hi, m_lo, start, stop):
                pe.matmul(acc, w_hi, m_hi, start=start, stop=False)
                pe.matmul(acc, w_hi, m_lo, start=False, stop=False)
                return pe.matmul(acc, w_lo, m_hi, start=False, stop=stop)

            def column(s, at):
                return w_high_buf[s][:, at:at + P], w_low_buf[s][:, at:at + P]

            def norm_stats(n):
                pe.wait_ge(norm_sum, 7 * (n + 1))
                for i in range(TT):
                    last = pe.matmul(O[3][:, 2 * i:2 * i + 2], ssum[:, i * P:(i + 1) * P], all_ones[:, :], start=True, stop=True)
                last.then_inc(norm_stat, 1)

            def norm_turn(n):
                pe.wait_ge(norm_spread, n + 1)
                for i in range(TT):
                    last = pe.transpose(O[2][:, i * P:(i + 1) * P], rexp[:, i * P:(i + 1) * P], ident[:, :])
                last.then_inc(norm_turned, 1)

            def in_unit(u, s, c, odd, h_base=None, hooks=(None, None)):
                pe.wait_ge(w_low, u + 1)
                for j in range(2):
                    acc = I[2 * odd + j]
                    cc = c + j
                    if hooks[j] is not None:
                        hooks[j]()
                    if not isinstance(cc, int) or cc >= 4:
                        pe.wait_ge(z_taken, cc - 3)
                    for kc in range(KC):
                        if h_base is not None and j == 0:
                            pe.wait_ge(h_low, h_base + kc + 1)
                        w_hi, w_lo = column(s, kc * 2 * P + j * P)
                        last = product(acc[:, :], w_hi, w_lo, h_high_buf[:, kc, :], h_low_buf[:, kc, :], kc == 0, kc == KC - 1)
                    last.then_inc(in_first if j == 0 else w_used, 1)

            def out_unit(u, s, q, n_units, acc, inputs, ready, x_wait):
                pe.wait_ge(w_low, u + 1)
                for kk in range(4):
                    k = 4 * q + kk
                    ready(k)
                    for m in range(4):
                        if k == 0:
                            x_wait(m)
                        w_hi, w_lo = column(s, kk * S + m * P)
                        last = product(acc[m][:, :], w_hi, w_lo, *inputs(k), k == 0, q == n_units - 1 and kk == 3)
                        if q == n_units - 1 and kk == 3 and m < 3:
                            last.then_inc(out_done, 1)
                last.then_inc(w_used, 1)

            def mlp(l):
                for half in range(2):
                    u0, c0 = U_MLP[l] + 16 * half, 32 * l + 16 * half
                    first = 0
                    if half == 0:
                        in_unit(u0, u0 % 2, c0, 0, h_base=H_MLP[l])
                        in_unit(u0 + 1, (u0 + 1) % 2, c0 + 2, 1,
                                hooks=(lambda: norm_stats(NORM_MLP[l]), lambda: norm_turn(NORM_MLP[l])))
                        first = 1
                    with pe.Fori(first, 4) as i:
                        for j in range(2):
                            in_unit(u0 + j + 2 * i, (u0 + j) % 2, c0 + 2 * j + 4 * i, j)

                    def ready(k):
                        pe.wait_ge(a_low, c0 + k + 1)

                    def inputs(k):
                        return a_high_buf[:, k, :], a_low_buf[:, k, :]

                    for f in range(NF):
                        def x_wait(m):
                            pe.wait_ge(x_ready, X_MLP[l] + 8 * half + 4 * f + m + 1 - 4)

                        for q in range(4):
                            u = u0 + 8 + 4 * f + q
                            out_unit(u, u % 2, q, 4, O, inputs, ready, x_wait)
                            if l == 1 and half == 1 and f == 1 and q == 0:
                                turn_result(0)

            def turn_result(f):
                pe.wait_ge(x_ready, X_MLP[1] + 8 + 4 * f + 4)
                for i in range(TT):
                    if f:
                        pe.wait_ge(y_copied[i % 2], i // 2 + 1)
                    for m in range(4):
                        last = pe.transpose(I[i][:, m * P:(m + 1) * P], xT[:, 4 * f + m, i * P:(i + 1) * P], ident[:, :])
                    last.then_inc(y_turned, 1)

            pe.wait_ge(consts_ready, 1)
            pe.wait_ge(params_landed, 16 * 9)
            pe.transpose(I[3][:, 0:N_PARAM], param_rows[0:N_PARAM, :], ident[0:N_PARAM, 0:N_PARAM]).then_inc(params_turned, 1)
            for i in range(TT):
                pe.wait_ge(x_landed[i], 16)
            for c in range(KC):
                if c >= 4:
                    pe.wait_ge(x_ready, c - 3)
                for i in range(TT):
                    last = pe.transpose(O[c % 4][:, i * P:(i + 1) * P], x_tok[:, i, c * P:(c + 1) * P], ident[:, :])
                last.then_inc(xt_done, 1)
            pe.wait_ge(const_steps, BAND_STEPS)
            pe.wait_ge(params_ready, 1)
            pe.wait_ge(h_tok_ready, TT)
            for c in range(KC):
                if c >= 4:
                    pe.wait_ge(h_low, c - 3)
                pe.matmul(I[c % 4][:, :], a_high_buf[:, 0, 0:P], a_high_buf[:, 0, :], start=True, stop=False)
                for i in range(TT):
                    n = min(BAND, S - i * P)
                    b = (band_first if i == 0 else band_rest)[:, c // (KC // G), 0:n]
                    last = pe.matmul(I[c % 4][:, i * P:i * P + n], h_tok[:, i, c * P:(c + 1) * P], b, start=False, stop=i == TT - 1)
                last.then_inc(mix_done, 1)
            pe.wait_ge(bias_in_landed, 32)
            pe.wait_ge(x_ready, 5)
            pe.matmul(O[0][0:H, :], rel_sb[:, :], bucket_sb[0:NB, :], start=True, stop=True).then_inc(bias_done, 1)
            pe.wait_ge(w_low, 1)
            for c in range(KC):
                g, d = c // (KC // G), c % (KC // G)
                if c < 4:
                    pe.wait_ge(h_low, max(2 * g + 2, 5 + c))
                else:
                    pe.wait_ge(x_ready, X_POOL + c - 3)
                for kc in range(GD // P):
                    w_hi, w_lo = column(0, (2 * g + kc) * GD + d * P)
                    last = product(I[c % 4][:, :], w_hi, w_lo, h_high_buf[:, 2 * g + kc, :], h_low_buf[:, 2 * g + kc, :],
                                   kc == 0, kc == GD // P - 1)
                last.then_inc(pool_done if c < KC - 1 else w_used, 1)
            pe.wait_ge(x_ready, X_POOL + KC - 3)
            mlp(0)

            def project(u, s, at, acc, hi, lo, done, chunks=range(KC), ready=None):
                for kc in chunks:
                    if ready is not None:
                        pe.wait_ge(h_low, ready + kc + 1)
                    w_hi, w_lo = column(s, at + kc * P)
                    last = product(acc[:, :], w_hi, w_lo, hi[:, kc, :], lo[:, kc, :], kc == 0, kc == KC - 1)
                if done is not None:
                    last.then_inc(done, 1)

            def kq_stats(n):
                pe.wait_ge(kq_sq, 2 * n + 2)
                for b, t in enumerate((ksq, qsq)):
                    for i in range(TT):
                        last = pe.matmul(I[3][:, 8 * b + 2 * i:8 * b + 2 * i + 2], t[:, i * P:(i + 1) * P], group_ones[:, :],
                                         start=True, stop=True)
                last.then_inc(kq_stat, 1)

            def o_stats(m, b):
                pe.wait_ge(o_copied, 2 * m + 2)
                for i in range(TT):
                    last = pe.matmul(b[:, 16 + 2 * i:18 + 2 * i], osq[:, i * P:(i + 1) * P], all_halves[:, :], start=True, stop=True)
                last.then_inc(o_stat, 1)

            def turn(src, b, ready, n, done):
                pe.wait_ge(ready, n + 1)
                for i in range(TT):
                    last = pe.transpose(b[:, i * P:(i + 1) * P], src[:, i * P:(i + 1) * P], ident[:, :])
                last.then_inc(done, 1)

            def scores(h, first):
                pe.wait_ge(kq_low, 3 * h + 3)
                if not first:
                    pe.wait_ge(at_low, 3 * h)
                    pe.wait_ge(o_copied, 2 * h)
                for j in range(2 * TT):
                    i, c = j // 2, j % 2
                    if j >= 4:
                        pe.wait_ge(s_taken, 8 * h + j - 3)
                    n, q = P * (i + 1), slice(i * P, (i + 1) * P)
                    product(O[j % 4][:, 0:n], q_hi[c][:, q], q_lo[c][:, q], k_hi[:, 0:n], k_lo[:, 0:n], True, True).then_inc(s_done, 1)

            def turn_probs(h):
                pe.wait_ge(s_taken, 8 * h + 8)
                for i in range(TT):
                    pe.wait_ge(a_ready, 4 * h + i + 1)
                    for j in range(i + 1):
                        b, at = AT_PLACE[j]
                        at += (i - j) * P
                        last = pe.transpose(O[b][:, at:at + P], p1(i)[:, j * P:(j + 1) * P], ident[:, :])
                last.then_inc(at_done, 1)

            def values(h):
                pe.wait_ge(at_low, 3 * h + 3)
                for j in range(TT):
                    b, at = AT_PLACE[j]
                    n = S - j * P
                    last = product(O[3][:, j * P:S], v_hi[:, j * P:(j + 1) * P], v_lo[:, j * P:(j + 1) * P],
                                   a_high_buf[:, 12 + b, at:at + n], a_low_buf[:, 12 + b, at:at + n], j == 0, j == TT - 1)
                last.then_inc(pv_done, 1)

            pe.wait_ge(w_low, U_HEAD + 1)
            project(U_HEAD, 1, 0, I[0], h_high_buf, h_low_buf, k_proj, ready=H_K)
            project(U_HEAD, 1, 1024, I[1], a_high_buf, a_low_buf, w_used, ready=H_Q)
            norm_stats(NORM_KV)
            norm_turn(NORM_KV)
            pe.wait_ge(w_low, U_HEAD + 2)
            project(U_HEAD + 1, 0, 0, I[2], h_high_buf, h_low_buf, w_used)
            kq_stats(0)
            turn(ksq, I[0], k_spread, 0, k_turned)
            turn(qsq, I[1], q_spread, 0, q_turned)
            turn(vf, I[2], vf_ready, 0, v_turned)
            pe.wait_ge(const_steps, BAND_STEPS + 4)

            def head(h, first):
                n = h + 1
                scores(h, first)
                pe.wait_ge(w_low, U_HEAD + 1 + 2 * n)
                project(None, 1, 0, I[0], h_high_buf, h_low_buf, k_proj)
                project(None, 1, 1024, I[1], a_high_buf, a_low_buf, w_used)
                turn_probs(h)
                pe.wait_ge(w_low, U_HEAD + 2 + 2 * n)
                pe.wait_ge(v_low, n)
                project(None, 0, 0, I[2], h_high_buf, h_low_buf, None, range(0, 4))
                if not first:
                    o_stats(h - 1, I[3])
                kq_stats(n)
                project(None, 0, 0, I[2], h_high_buf, h_low_buf, w_used, range(4, KC))
                if not first:
                    turn(osq, O[3], o_spread, h - 1, o_turned)
                turn(ksq, I[0], k_spread, n, k_turned)
                turn(qsq, I[1], q_spread, n, q_turned)
                if not first:
                    pe.wait_ge(o_ready, h)
                values(h)
                turn(vf, I[2], vf_ready, n, v_turned)

            head(0, True)
            with pe.Fori(1, H - 1) as h:
                head(h, False)

            last_h = H - 1
            scores(last_h, False)
            o_stats(last_h - 1, I[3])
            pe.wait_ge(v_low, H)

            def wo_part(u, q, f, kks):
                acc = I if f == 0 else O
                for kk in kks:
                    k = 4 * q + kk
                    pe.wait_ge(h_low, H_O + k + 1)
                    for m in range(4):
                        if k == 0 and f == 0 and m == 3:
                            pe.wait_ge(o_rooted, H - 1)
                        w_hi, w_lo = column(u % 2, kk * S + m * P)
                        last = product(acc[m][:, :], w_hi, w_lo, h_high_buf[:, k, :], h_low_buf[:, k, :], k == 0, k == KC - 1)
                        if k == KC - 1 and m < 3:
                            last.then_inc(out_done, 1)
                return last

            pe.wait_ge(w_low, U_WO + 1)
            wo_part(U_WO, 0, 0, range(4)).then_inc(w_used, 1)
            turn(osq, O[3], o_spread, last_h - 1, o_turned)
            turn_probs(last_h)
            pe.wait_ge(w_low, U_WO + 2)
            wo_part(U_WO + 1, 1, 0, [0])
            pe.wait_ge(o_ready, last_h)
            values(last_h)
            wo_part(U_WO + 1, 1, 0, [1])
            o_stats(last_h, O[0])
            wo_part(U_WO + 1, 1, 0, [2])
            turn(osq, O[1], o_spread, last_h, o_turned)
            wo_part(U_WO + 1, 1, 0, [3]).then_inc(w_used, 1)
            for q in range(2):
                pe.wait_ge(w_low, U_WO + 3 + q)
                wo_part(U_WO + 2 + q, q, 1, range(4)).then_inc(w_used, 1)
            mlp(1)
            turn_result(1)


_INS = ["x", "norm_mix", "norm_mlp", "pool_w", "pool_scale", "kv_norm", "w_kv", "k_norm", "rel_bias", "w_q", "q_norm",
        "lam_q1", "lam_k1", "lam_q2", "lam_k2", "subln", "w_o", "w_mlp_in", "w_mlp_out"]


def kernel(**inputs):
    import concourse.bacc as bacc
    from concourse.bass_utils import run_bass_kernel_spmd

    nc = bacc.Bacc("TRN2", target_bir_lowering=False, num_devices=1)
    arrays = {name: np.ascontiguousarray(inputs[name]) for name in _INS}
    arrays["bucket_rows"] = distance_buckets()
    args = [nc.dram_tensor(f"in_{n}_dram", a.shape, mybir.dt.from_np(a.dtype), kind="ExternalInput").ap() for n, a in arrays.items()]
    out = nc.dram_tensor("out_0_dram", (1, S, D), mybir.dt.float32, kind="ExternalOutput").ap()
    build_program(nc, *args, out)
    r = run_bass_kernel_spmd(nc, [{f"in_{n}_dram": a for n, a in arrays.items()}], core_ids=[0])
    return r.results[0]["out_0_dram"]
```

```python
import math

import numpy as np

import concourse.bass as bass
from concourse import mybir
from contextlib import ExitStack

D = 1024
S = 512
P = 128
KC = D // P
TT = S // P
WINDOWS = (2, 4, 8, 16)
G = len(WINDOWS)
GD = D // G
H = 8
HD = D // (2 * H)
FF = 4 * D
NB = 32
MAXD = 128
EPS = 1e-6
LAMBDA_INIT = 0.8 - 0.6 * math.exp(-0.3)
MASKED = -3.0e38
REL = 640
BAND = P + max(WINDOWS) - 1

UNIT = 2048
U_POOL = 0
U_MLP = (1, 53)
U_HEAD = 33
U_WO = 49
UNITS = 85
NF = 2
HALF_CHUNKS = FF // P // 2

C_MIX, C_MLP, C_PSCALE, C_KV, C_QN, C_KN, C_SUB = 0, 16, 32, 40, 48, 49, 50
N_PARAM = 51


def distance_buckets():
    rel = np.arange(S - 1, -1, -1)
    exact = NB // 2
    nf = np.maximum(rel, 1).astype(np.float32)
    large = exact + (np.log(nf / np.float32(exact)) / np.float32(math.log(MAXD / exact)) * np.float32(NB - exact)).astype(np.int32)
    bucket = np.where(rel < exact, rel, np.minimum(large, NB - 1))
    return (np.arange(NB)[:, None] == bucket[None, :]).astype(np.float32)


def pooling_bands():
    bands = np.zeros((P, 2, G, BAND), np.float32)
    for g, w in enumerate(WINDOWS):
        for p in range(P):
            for n in range(p, min(p + w, BAND)):
                bands[p, 0, g, n] = np.float32(1) / np.float32(min(w, n + 1))
                bands[p, 1, g, n] = np.float32(1) / np.float32(w)
            bands[p, :, g, p] -= np.float32(1)
    return bands


def build_program(nc, x, norm_mix, norm_mlp, pool_w, pool_scale, kv_norm, w_kv, k_norm, rel_bias,
                  w_q, q_norm, lam_q1, lam_k1, lam_q2, lam_k2, subln, w_o, w_mlp_in, w_mlp_out,
                  bucket_rows, bands, out):
    F32, F32R = mybir.dt.float32, mybir.dt.float32r
    ALU, ACT = mybir.AluOpType, mybir.ActivationFunctionType
    ctx = ExitStack()
    with ctx:
        def sb(name, shape, dt=F32):
            return ctx.enter_context(nc.sbuf_tensor(name, shape, dt))

        def sem(name):
            return ctx.enter_context(nc.semaphore(name))

        xT = sb("xT", [P, KC, S])
        raw = [sb(f"raw{i}", [P, UNIT]) for i in range(2)]
        w_high_buf = [sb(f"w_high{i}", [P, UNIT], F32R) for i in range(2)]
        w_low_buf = [sb(f"w_low{i}", [P, UNIT], F32R) for i in range(2)]
        h_high_buf = sb("h_high_buf", [P, KC, S], F32R)
        h_low_buf = sb("h_low_buf", [P, KC, S], F32R)
        a_high_buf = sb("a_high_buf", [P, HALF_CHUNKS, S], F32R)
        a_low_buf = sb("a_low_buf", [P, HALF_CHUNKS, S], F32R)
        work = sb("work", [P, 11008])
        ident = sb("ident", [P, P])
        params = sb("params", [P, N_PARAM])
        group_ones = sb("group_ones", [P, 2])
        all_ones = sb("all_ones", [P, 2])
        all_halves = sb("all_halves", [P, 2])
        eps = sb("eps", [P, 1])
        qk_gain = sb("qk_gain", [P, 1])
        sub_gain = sb("sub_gain", [P, 1])
        rel_sb = sb("rel_sb", [NB, H])
        tok_ss = sb("tok_ss", [P, TT])
        tok_root = sb("tok_root", [P, TT])
        tok_rstd = sb("tok_rstd", [P, TT])
        norm_root = sb("norm_root", [P, 2 * TT])
        norm_rstd = sb("norm_rstd", [P, TT])
        lam_dots = sb("lam_dots", [P, 2])
        lam_exps = sb("lam_exps", [P, 2])
        neg_lam = sb("neg_lam", [P, 1])
        wait_cell = sb("wait_cell", [1, TT])
        table_cell = sb("table_cell", [P, 1])
        row_max = sb("row_max", [P, 8])
        neg_max = sb("neg_max", [P, 8])
        row_sum = sb("row_sum", [P, 8])
        row_inv = sb("row_inv", [P, 8])
        kq_root_buf = sb("kq_root_buf", [P, 16])
        kq_rstd_buf = sb("kq_rstd_buf", [P, 16])
        o_root_buf = sb("o_root_buf", [P, 2 * TT])
        o_rstd_buf = sb("o_rstd_buf", [P, TT])

        def region(at, n):
            return work[:, at:at + n]

        kf, qf, vf = (region(i * S, S) for i in range(3))
        ksq, qsq, osq = (region((3 + i) * S, S) for i in range(3))
        of = region(3072, S)
        bias_tile = region(3584, S)
        p1_all = region(4096, 1280)
        p2_ring = [region(5376 + i * S, S) for i in range(2)]
        o_all = region(6400, H * S).rearrange("p (h t) -> p h t", h=H)
        rstd_bc = region(10496, S)
        relu_buf = [region(i * S, S) for i in range(2)]
        sq_buf = [region(1024 + i * S, S) for i in range(2)]
        ring = [region(2048 + i * S, S) for i in range(2)]
        ssum = region(3072, S)
        rexp = region(4096, S)
        out_sb = region(6400, TT * D).rearrange("p (i d) -> p i d", i=TT)
        x_tok = region(0, TT * D).rearrange("p (i d) -> p i d", i=TT)
        h_tok = region(4096, TT * D).rearrange("p (i d) -> p i d", i=TT)
        band_sb = region(8192, 2 * G * BAND).rearrange("p (f g n) -> p f g n", f=2, g=G)
        param_rows = region(9344, P)
        bucket_sb = region(9472, S)
        bias_rows = region(9984, REL)
        lam_sb = region(10624, 4 * HD).rearrange("p (v d) -> p v d", v=4)
        lam_junk = region(10880, HD)

        P1_AT = [0, 128, 384, 768]

        def p1(i):
            return p1_all[:, P1_AT[i]:P1_AT[i] + P * (i + 1)]

        m_high_buf, m_low_buf = a_high_buf[:, KC:2 * KC, :], a_low_buf[:, KC:2 * KC, :]
        ACT_CHUNKS, DVE_CHUNKS = (4, 5, 6, 7, 0), (1, 2, 3)

        k_hi, k_lo = a_high_buf[:, 8, :], a_low_buf[:, 8, :]
        q_hi, q_lo = [a_high_buf[:, 9 + c, :] for c in range(2)], [a_low_buf[:, 9 + c, :] for c in range(2)]
        v_hi, v_lo = a_high_buf[:, 11, :], a_low_buf[:, 11, :]
        w_o_high, w_o_low = a_high_buf[:, 0:KC, :], a_low_buf[:, 0:KC, :]
        AT_PLACE = [(0, 0), (1, 0), (2, 0), (1, 384)]
        AT_COLS = [512, 512, 256]

        bank = [ctx.enter_context(nc.psum_tensor(f"bank{i}", [P, S], F32)) for i in range(8)]
        O, I = bank[0:4], bank[4:8]

        scratch = nc.dram_tensor("bias_by_distance", (H, P, REL), F32, kind="Internal").ap()

        x_landed = [sem(f"x_landed{i}") for i in range(TT)]
        bands_landed = sem("bands_landed")
        params_landed = sem("params_landed")
        lam_landed = sem("lam_landed")
        bias_in_landed = sem("bias_in_landed")
        w_landed = [sem(f"w_landed{i}") for i in range(2)]
        bias_stored = sem("bias_stored")
        t_landed = sem("t_landed")
        out_stored = sem("out_stored")
        w_high = sem("w_high")
        w_low = sem("w_low")
        first_low = sem("first_low")
        w_used = sem("w_used")
        consts_ready = sem("consts_ready")
        const_steps = sem("const_steps")
        params_turned = sem("params_turned")
        params_ready = sem("params_ready")
        bias_done = sem("bias_done")
        bias_rows_ready = sem("bias_rows_ready")
        tok_sq = sem("tok_sq")
        tok_rooted = sem("tok_rooted")
        tok_inverse = sem("tok_inverse")
        h_tok_ready = sem("h_tok_ready")
        xt_done = sem("xt_done")
        xt_copied = sem("xt_copied")
        mix_done = sem("mix_done")
        pool_done = sem("pool_done")
        lam_dot = sem("lam_dot")
        lam_exp = sem("lam_exp")
        lam_ready = sem("lam_ready")
        x_ready = sem("x_ready")
        h_high = sem("h_high")
        h_low = sem("h_low")
        norm_sq = sem("norm_sq")
        norm_sum = sem("norm_sum")
        norm_stat = sem("norm_stat")
        norm_rooted = sem("norm_rooted")
        norm_inverse = sem("norm_inverse")
        norm_spread = sem("norm_spread")
        norm_turned = sem("norm_turned")
        rstd_ready = sem("rstd_ready")
        in_first = sem("in_first")
        z_taken = sem("z_taken")
        z_squared = sem("z_squared")
        a_high = sem("a_high")
        a_low = sem("a_low")
        out_done = sem("out_done")
        k_proj = sem("k_proj")
        kf_ready = sem("kf_ready")
        qf_ready = sem("qf_ready")
        vf_ready = sem("vf_ready")
        kq_sq = sem("kq_sq")
        kq_stat = sem("kq_stat")
        kq_rooted = sem("kq_rooted")
        kq_inverse = sem("kq_inverse")
        k_spread = sem("k_spread")
        q_spread = sem("q_spread")
        k_turned = sem("k_turned")
        q_turned = sem("q_turned")
        kn_ready = sem("kn_ready")
        qn_ready = sem("qn_ready")
        kq_high = sem("kq_high")
        kq_low = sem("kq_low")
        v_turned = sem("v_turned")
        v_high = sem("v_high")
        v_low = sem("v_low")
        s_done = sem("s_done")
        s_taken = sem("s_taken")
        max_ready = sem("max_ready")
        table_in = sem("table_in")
        exp_done = sem("exp_done")
        inv_ready = sem("inv_ready")
        second_scaled = sem("second_scaled")
        a_ready = sem("a_ready")
        at_done = sem("at_done")
        at_high = sem("at_high")
        at_low = sem("at_low")
        pv_done = sem("pv_done")
        o_copied = sem("o_copied")
        o_stat = sem("o_stat")
        o_rooted = sem("o_rooted")
        o_inverse = sem("o_inverse")
        o_spread = sem("o_spread")
        o_turned = sem("o_turned")
        o_ready = sem("o_ready")
        y_turned = sem("y_turned")
        y_copied = [sem(f"y_copied{i}") for i in range(2)]

        CONST_STEPS = 8
        X_POOL = len(DVE_CHUNKS)
        X_MLP, X_WO = (X_POOL + 8, X_POOL + 32), X_POOL + 24
        H_POOL, H_MLP, H_K, H_Q, H_O = 0, (8, 40), 16, 24, 32
        OUT_MLP, OUT_WO = (0, 18), 12
        NORM_MLP, NORM_KV = (0, 2), 1

        def landed(u0, i=0):
            count = 16 * (u0 // 2 + 1)
            if u0 % 2 and u0 >= U_WO:
                count += 16 * H + 16
            return count + 16 * i

        def head_landed(n):
            return 16 * (U_HEAD // 2) + 32 * (n + 1)

        pool_v = pool_w[0].rearrange("g (k p) n -> p g k n", p=P)
        wk_v = w_kv.rearrange("(k p) n -> p k n", p=P)
        wq_v = w_q[0].rearrange("(k p) n -> p k n", p=P)
        wo_v = w_o[0].rearrange("(k p) n -> p k n", p=P)
        win_v = [w_mlp_in[l].rearrange("(k p) n -> p k n", p=P) for l in range(2)]
        wout_v = [w_mlp_out[l].rearrange("(k p) n -> p k n", p=P) for l in range(2)]

        def tile3(t, k):
            return t[:, :].rearrange("p (k n) -> p k n", k=k)

        block = ctx.enter_context(nc.Block())

        @block.sync
        def _(sp):
            for i in range(TT):
                sp.dma_start(x_tok[:, i, :], x[0, i * P:(i + 1) * P, :]).then_inc(x_landed[i], 16)
            sp.dma_start(band_sb, bands).then_inc(bands_landed, 16)
            sp.dma_start(param_rows[0:16, :], norm_mix.rearrange("l (k p) -> (l k) p", p=P)).then_inc(params_landed, 16)
            sp.dma_start(param_rows[16:32, :], norm_mlp.rearrange("l (k p) -> (l k) p", p=P)).then_inc(params_landed, 16)
            sp.dma_start(param_rows[32:40, :], pool_scale[0].rearrange("(k p) -> k p", p=P)).then_inc(params_landed, 16)
            sp.dma_start(param_rows[40:48, :], kv_norm.rearrange("(k p) -> k p", p=P)).then_inc(params_landed, 16)
            sp.dma_start(param_rows[48:49, :].rearrange("a (c d) -> a c d", c=2), q_norm[0:1, :].unsqueeze(1).to_broadcast([1, 2, HD]))\
              .then_inc(params_landed, 16)
            sp.dma_start(param_rows[49:50, :].rearrange("a (c d) -> a c d", c=2),
                         k_norm.rearrange("(a d) -> a d", a=1).unsqueeze(1).to_broadcast([1, 2, HD])).then_inc(params_landed, 16)
            sp.dma_start(param_rows[50:51, :], subln[0:1, :]).then_inc(params_landed, 16)
            sp.dma_start(raw[0][:, :].rearrange("p (g k n) -> p g k n", g=G, k=GD // P), pool_v).then_inc(w_landed[0], 16)

            sp.dma_start(tile3(raw[1], KC), win_v[0][:, :, 0:2 * P]).then_inc(w_landed[1], 16)
            sp.dma_start(bucket_sb[0:NB, :], bucket_rows).then_inc(bias_in_landed, 16)
            sp.dma_start(rel_sb[:, :], rel_bias).then_inc(bias_in_landed, 16)
            for v, lam in enumerate((lam_q1, lam_k1, lam_q2, lam_k2)):
                sp.dma_start(lam_sb[:, v, :], lam[0:1, :].to_broadcast([P, HD])).then_inc(lam_landed, 16)

            def slot_free(u):
                sp.wait_ge(w_low, u - 1)

            def load_in(l, u, s, column):
                slot_free(u)
                sp.dma_start(tile3(raw[s], KC), win_v[l][:, :, bass.ds(column, 2 * P)]).then_inc(w_landed[s], 16)

            def load_mlp(l):
                for half in range(2):
                    u0 = U_MLP[l] + 16 * half
                    if l == 0 and half == 0:
                        load_in(l, u0 + 1, 0, 2 * P)
                        first = 1
                    else:
                        first = 0
                    with sp.Fori(first, 4) as i:
                        for j in range(2):
                            load_in(l, u0 + 2 * i + j, (u0 + j) % 2, half * 2048 + 512 * i + 256 * j)
                    for f in range(NF):
                        with sp.Fori(0, 2) as r:
                            for j in range(2):
                                u = u0 + 8 + 4 * f + j
                                slot_free(u + 2 * r)
                                sp.dma_start(tile3(raw[u % 2], 4),
                                             wout_v[l][:, bass.ds(half * HALF_CHUNKS + 8 * r + 4 * j, 4), f * S:(f + 1) * S])\
                                  .then_inc(w_landed[u % 2], 16)

            load_mlp(0)
            with sp.Fori(0, H) as n:
                slot_free(U_HEAD + 2 * n)
                sp.dma_start(tile3(raw[1][:, 0:1024], KC), wk_v[:, :, bass.ds(n * P, P)]).then_inc(w_landed[1], 16)
                sp.dma_start(tile3(raw[1][:, 1024:2048], KC), wq_v[:, :, bass.ds(n * P, P)]).then_inc(w_landed[1], 16)
                slot_free(U_HEAD + 1 + 2 * n)
                sp.dma_start(tile3(raw[0][:, 0:1024], KC), wk_v[:, :, bass.ds(D + n * P, P)]).then_inc(w_landed[0], 16)
            for f in range(NF):
                for q in range(2):
                    u = U_WO + 2 * f + q
                    slot_free(u)
                    if u == U_WO:
                        for b in range(2):
                            sp.dma_start(tile3(raw[1][:, b * 1024:(b + 1) * 1024], 2),
                                         wo_v[:, 2 * b:2 * b + 2, 0:S]).then_inc(w_landed[1], 16)
                    else:
                        sp.dma_start(tile3(raw[u % 2], 4), wo_v[:, 4 * q:4 * q + 4, f * S:(f + 1) * S])\
                          .then_inc(w_landed[u % 2], 16)
            load_mlp(1)
            for f in range(NF):
                for i in range(TT):
                    sp.wait_ge(y_copied[i % 2], 2 * f + i // 2 + 1)
                    sp.dma_start(out[0, i * P:(i + 1) * P, f * S:(f + 1) * S], out_sb[:, i, f * S:(f + 1) * S])\
                      .then_inc(out_stored, 16)
            sp.wait_ge(out_stored, 16 * NF * TT)

        @block.gpsimd
        def _(pool):
            steps = [0]

            def done(instruction):
                steps[0] += 1
                instruction.then_inc(const_steps, 1)
                pool.wait_ge(const_steps, steps[0])

            done(pool.memset(ident[:, :], 0.0))
            done(pool.affine_select(out=ident[:, :], in_=ident[:, :], compare_op=ALU.not_equal, fill=1.0, base=0,
                                    pattern=[[-1, P]], channel_multiplier=1))
            done(pool.memset(all_ones[:, :], 1.0))
            done(pool.memset(a_high_buf[:, 0, :].bitcast(F32), 0.0))
            done(pool.memset(all_halves[:, :], 0.5))
            done(pool.memset(group_ones[:, :], 0.0))
            done(pool.memset(group_ones[0:HD, 0:1], 1.0))
            done(pool.memset(group_ones[HD:P, 1:2], 1.0))
            pool.memset(eps[:, :], EPS).then_inc(consts_ready, 1)
            pool.wait_ge(w_high, 2)
            pool.tensor_tensor(w_low_buf[1][:, :], raw[1][:, :], w_high_buf[1][:, :].bitcast(F32), ALU.subtract).then_inc(first_low, 1)
            pool.wait_ge(bias_rows_ready, 2)
            pool.dma_start(scratch, bias_rows[0:H, :].unsqueeze(1).to_broadcast([H, P, REL])).then_inc(bias_stored, 16)
            pool.wait_ge(bias_stored, 16)
            pool.wait_ge(w_used, U_HEAD)
            for q in (q_hi, q_lo):
                done(pool.memset(q[0][HD:P, :].bitcast(F32), 0.0))
                done(pool.memset(q[1][0:HD, :].bitcast(F32), 0.0))
            for h in range(H):
                if h:
                    pool.wait_ge(s_taken, 8 * h)
                pool.dma_start(bias_tile, bass.AP(tensor=scratch.tensor, offset=h * P * REL + P - 1, ap=[[REL - 1, P], [1, S]]))\
                    .then_inc(t_landed, 16)

        @block.scalar
        def _(act):
            def split_high(u, s, landed_count, cols=UNIT):
                act.wait_ge(w_landed[s], landed_count)
                if not isinstance(u, int) or u >= 2:
                    act.wait_ge(w_used, u - 1)
                act.activation(w_high_buf[s][:, 0:cols], raw[s][:, 0:cols], ACT.Copy).then_inc(w_high, 1)

            def input_high(dst, src, gain):
                act.activation(dst, src, ACT.Copy, scale=gain).then_inc(h_high, 1)

            def norm_squares(n, chunks=range(KC)):
                for c in chunks:
                    if c >= 3:
                        act.wait_ge(norm_sum, 7 * n + c - 2)
                    act.activation(ssum if c == 0 else ring[(c - 1) % 2], xT[:, c, :], ACT.Square).then_inc(norm_sq, 1)

            def norm_root_step(n):
                act.wait_ge(norm_stat, n + 1)
                act.activation(norm_root[:, :], O[3][:, 0:2 * TT], ACT.Sqrt, scale=1.0 / D, bias=eps[:, 0:1])\
                   .then_inc(norm_rooted, 1)

            def prep_x(h_base, x_base, dst, gain, chunks=range(KC)):
                for c in chunks:
                    act.wait_ge(x_ready, x_base + c + 1)
                    input_high(dst[:, c, :], xT[:, c, :], params[:, gain + c:gain + c + 1])

            def hidden(c, k):
                for j in range(2):
                    cc, kk = c + j, k + j
                    s = j
                    act.wait_ge(z_taken, cc + 1)
                    if not isinstance(cc, int) or cc >= 2:
                        act.wait_ge(a_low, cc - 1)
                    act.activation(sq_buf[s], relu_buf[s], ACT.Square).then_inc(z_squared, 1)
                    act.wait_ge(z_squared, cc + 1)
                    act.activation(a_high_buf[:, bass.ds(kk, 1), :] if not isinstance(kk, int) else a_high_buf[:, kk, :],
                                   sq_buf[s], ACT.Copy).then_inc(a_high, 1)

            def mlp(l):
                for half in range(2):
                    u0, c0 = U_MLP[l] + 16 * half, 32 * l + 16 * half
                    first = 0
                    if half == 0:
                        split_high(u0 + 1, (u0 + 1) % 2, landed(u0 + 1))
                        norm_squares(NORM_MLP[l], range(0 if l == 0 else 4, KC))
                        split_high(u0 + 2, u0 % 2, landed(u0 + 2))
                        norm_root_step(NORM_MLP[l])
                        hidden(c0, 0)
                        hidden(c0 + 2, 2)
                        first = 1
                    with act.Fori(first, 4) as i:
                        for j in range(2):
                            split_high(u0 + 1 + j + 2 * i, (u0 + 1 + j) % 2, landed(u0 + 1 + j, i))
                            hidden(c0 + 2 * j + 4 * i, 2 * j + 4 * i)
                    for f in range(NF):
                        u = u0 + 8 + 4 * f + 1
                        if half == 1 and f == 1:
                            for q in range(3):
                                split_high(u + q, (u + q) % 2, landed(u + q))
                                if l == 0 and q == 0:
                                    prep_x(H_K, X_MLP[0] + 8, h_high_buf, C_KV, range(4))
                                    norm_squares(NORM_KV, range(4))
                            if l == 0:
                                split_high(U_HEAD, 1, head_landed(0))
                        else:
                            with act.Fori(0, 2) as r:
                                for j in range(2):
                                    split_high(u + j + 2 * r, (u + j) % 2, landed(u + j, r))

            act.wait_ge(consts_ready, 1)
            act.activation(tok_root[:, 0:1], eps[:, :], ACT.Sqrt).then_inc(tok_sq, 1)
            for i in range(TT):
                act.wait_ge(x_landed[i], 16)
                act.activation(h_tok[:, i, :], x_tok[:, i, :], ACT.Square, accum_out=tok_ss[:, i:i + 1]).then_inc(tok_sq, 1)
            act.wait_ge(tok_sq, TT + 1)
            act.activation(tok_root[:, :], tok_ss[:, :], ACT.Sqrt, scale=1.0 / D, bias=eps[:, 0:1]).then_inc(tok_rooted, 1)
            act.wait_ge(xt_done, TT)
            for n, c in enumerate(ACT_CHUNKS):
                if n == TT:
                    act.wait_ge(params_turned, 1)
                    act.activation(params[:, :], I[0][:, 0:N_PARAM], ACT.Copy).then_inc(params_ready, 1)
                act.activation(xT[:, c, :], bank[c][:, :], ACT.Copy).then_inc(xt_copied, 1)
            split_high(0, 0, 16)
            act.wait_ge(params_ready, 1)
            for c in range(KC):
                act.wait_ge(mix_done, c + 1)
                input_high(m_high_buf[:, c, :], I[c % 4][:, :], params[:, C_MIX + c:C_MIX + c + 1])
                if c == 4:
                    split_high(1, 1, 16)
                if c == 6:
                    act.wait_ge(bias_done, 1)
                    act.activation(bias_rows[0:H, 0:S], O[0][0:H, :], ACT.Copy).then_inc(bias_rows_ready, 1)
            act.wait_ge(lam_dot, 2)
            act.activation(lam_exps[:, :], lam_dots[:, :], ACT.Exp).then_inc(lam_exp, 1)
            prep_x(H_MLP[0], X_POOL, h_high_buf, C_MLP)
            mlp(0)

            def project(n):
                act.wait_ge(kf_ready, n + 1)
                act.activation(ksq, kf, ACT.Square).then_inc(kq_sq, 1)

            def project_q(n):
                act.wait_ge(qf_ready, n + 1)
                act.activation(qsq, qf, ACT.Square).then_inc(kq_sq, 1)

            def kq_roots(n):
                act.wait_ge(kq_stat, n + 1)
                act.activation(kq_root_buf[:, :], I[3][:, 0:16], ACT.Sqrt, scale=1.0 / HD, bias=eps[:, 0:1]).then_inc(kq_rooted, 1)

            def kq_highs(n):
                act.wait_ge(kn_ready, n + 1)
                act.activation(k_hi, kf, ACT.Copy).then_inc(kq_high, 1)
                act.wait_ge(qn_ready, n + 1)
                for c in range(2):
                    r = slice(c * HD, (c + 1) * HD)
                    act.activation(q_hi[c][r, :], qf[r, :], ACT.Copy, scale=qk_gain[r, 0:1]).then_inc(kq_high, 1)

            def v_highs(n):
                act.wait_ge(v_turned, n + 1)
                act.activation(v_hi, I[2][:, :], ACT.Copy).then_inc(v_high, 1)

            def bring_table(f):
                act.activation(table_cell[:, :], eps[:, :], f).then_inc(table_in, 1)

            def exps(h, tiles=range(TT)):
                for i in tiles:
                    act.wait_ge(max_ready, 4 * h + i + 1)
                    for c in range(2):
                        t = p1(i) if c == 0 else p2_ring[i % 2][:, 0:P * (i + 1)]
                        act.activation(t, t, ACT.Exp, bias=neg_max[:, 2 * i + c:2 * i + c + 1],
                                       accum_out=row_sum[:, 2 * i + c:2 * i + c + 1]).then_inc(exp_done, 1)

            def at_highs(h):
                act.wait_ge(at_done, h + 1)
                for b in range(3):
                    act.activation(a_high_buf[:, 12 + b, 0:AT_COLS[b]], O[b][:, 0:AT_COLS[b]], ACT.Copy).then_inc(at_high, 1)

            def o_roots(m, b):
                act.wait_ge(o_stat, m + 1)
                act.activation(o_root_buf[:, :], b[:, 16:16 + 2 * TT], ACT.Sqrt, scale=1.0 / HD, bias=eps[:, 0:1]).then_inc(o_rooted, 1)

            def o_copies(h):
                act.wait_ge(pv_done, h + 1)
                act.activation(of, O[3][:, :], ACT.Copy).then_inc(o_copied, 1)
                act.activation(osq, O[3][:, :], ACT.Square).then_inc(o_copied, 1)

            def o_high(k):
                act.wait_ge(o_ready, k + 1)
                input_high(w_o_high[:, k, :], o_all[:, k, :], sub_gain[:, 0:1])

            prep_x(H_K, X_MLP[0] + 8, h_high_buf, C_KV, range(4, KC))
            norm_squares(NORM_KV, range(4, KC))
            prep_x(H_Q, X_MLP[0] + 8, a_high_buf, C_MIX + KC, range(4))
            norm_root_step(NORM_KV)
            prep_x(H_Q, X_MLP[0] + 8, a_high_buf, C_MIX + KC, range(4, KC))
            split_high(U_HEAD + 1, 0, landed(U_HEAD + 1), 1024)
            project(0)
            project_q(0)
            kq_roots(0)
            bring_table(ACT.Exp)
            kq_highs(0)
            split_high(U_HEAD + 2, 1, head_landed(1))
            v_highs(0)

            def head(h, first):
                exps(h)
                bring_table(ACT.Sqrt)
                split_high(U_HEAD + 3 + 2 * h, 0, landed(U_HEAD + 3, h), 1024)
                project(h + 1)
                project_q(h + 1)
                at_highs(h)
                kq_roots(h + 1)
                if not first:
                    o_roots(h - 1, I[3])
                bring_table(ACT.Exp)
                kq_highs(h + 1)
                split_high(U_HEAD + 4 + 2 * h, 1, head_landed(h + 2))
                o_copies(h)
                v_highs(h + 1)

            head(0, True)
            with act.Fori(1, H - 1) as h:
                head(h, False)
            act.wait_ge(w_used, U_WO - 1)
            o_high(0)
            for i in range(TT):
                exps(H - 1, [i])
                if i < 3:
                    o_high(i + 1)
                if i == 1:
                    split_high(U_WO + 1, 0, landed(U_WO + 1))
            o_roots(H - 2, I[3])
            o_high(4)
            at_highs(H - 1)
            o_high(5)
            o_high(6)
            split_high(U_WO + 2, 1, landed(U_WO + 2))
            o_copies(H - 1)
            o_roots(H - 1, O[0])
            o_high(7)
            split_high(U_WO + 3, 0, landed(U_WO + 3))
            prep_x(H_MLP[1], X_WO, h_high_buf, C_MLP + KC, range(4))
            norm_squares(NORM_MLP[1], range(4))
            split_high(U_WO + 4, 1, landed(U_WO + 4))
            prep_x(H_MLP[1], X_WO, h_high_buf, C_MLP + KC, range(4, KC))

            def copy_result(f):
                for i in (0, 2):
                    act.wait_ge(y_turned, 4 * f + i + 1)
                    act.activation(out_sb[:, i, f * S:(f + 1) * S], I[i][:, :], ACT.Copy).then_inc(y_copied[0], 1)

            mlp(1)
            for f in range(NF):
                copy_result(f)

        @block.vector
        def _(dve):
            def f32(t):
                return t.bitcast(F32)

            def split_low(u, s, cols=UNIT):
                dve.wait_ge(w_high, u + 1)
                dve.tensor_tensor(w_low_buf[s][:, 0:cols], raw[s][:, 0:cols], f32(w_high_buf[s][:, 0:cols]), ALU.subtract)\
                   .then_inc(w_low, 1)

            def input_low(dst, src, gain, high):
                dve.scalar_tensor_tensor(dst, src, gain, f32(high), ALU.mult, ALU.subtract).then_inc(h_low, 1)

            def prep_x(h_base, hi, lo, gain, chunks=range(KC)):
                for c in chunks:
                    dve.wait_ge(h_high, h_base + c + 1)
                    input_low(lo[:, c, :], xT[:, c, :], params[:, gain + c:gain + c + 1], hi[:, c, :])

            def norm_sums(n, chunks=range(1, KC)):
                for c in chunks:
                    dve.wait_ge(norm_sq, 8 * n + c + 1)
                    if c > 1:
                        dve.wait_ge(norm_sum, 7 * n + c - 1)
                    dve.tensor_tensor(ssum, ssum, ring[(c - 1) % 2], ALU.add).then_inc(norm_sum, 1)

            def norm_invert(n):
                dve.wait_ge(norm_rooted, n + 1)
                dve.reciprocal(norm_rstd[:, :], norm_root[:, :].rearrange("p (i b) -> p i b", b=2)[:, :, 0]).then_inc(norm_inverse, 1)
                dve.wait_ge(norm_inverse, n + 1)
                dve.tensor_copy(rexp.rearrange("p (i n) -> p i n", i=TT), norm_rstd[:, :].unsqueeze(2).to_broadcast([P, TT, P]))\
                   .then_inc(norm_spread, 1)

            def norm_keep(n):
                dve.wait_ge(norm_turned, n + 1)
                dve.tensor_copy(rstd_bc, O[2][:, :]).then_inc(rstd_ready, 1)
                dve.wait_ge(rstd_ready, n + 1)

            def hidden(u, n_in, c, k, odd):
                for j in range(2):
                    cc, kk = c + j, k + j
                    if j == 0:
                        dve.wait_ge(in_first, n_in + 1)
                    else:
                        dve.wait_ge(w_used, u + 1)
                    if not isinstance(cc, int) or cc >= 2:
                        dve.wait_ge(z_squared, cc - 1)
                    dve.scalar_tensor_tensor(relu_buf[j], I[2 * odd + j][:, :], 0.0, rstd_bc, ALU.max, ALU.mult)\
                       .then_inc(z_taken, 1)
                    dve.wait_ge(a_high, cc + 1)
                    hi = a_high_buf[:, kk, :] if isinstance(kk, int) else a_high_buf[:, bass.ds(kk, 1), :]
                    lo = a_low_buf[:, kk, :] if isinstance(kk, int) else a_low_buf[:, bass.ds(kk, 1), :]
                    dve.tensor_tensor(lo, sq_buf[j], f32(hi), ALU.subtract).then_inc(a_low, 1)

            def mlp(l):
                for half in range(2):
                    u0, c0 = U_MLP[l] + 16 * half, 32 * l + 16 * half
                    n0 = 16 * l + 8 * half
                    first = 0
                    if half == 0:
                        split_low(u0 + 1, (u0 + 1) % 2)
                        norm_sums(NORM_MLP[l], range(1 if l == 0 else 4, KC))
                        split_low(u0 + 2, u0 % 2)
                        norm_invert(NORM_MLP[l])
                        norm_keep(NORM_MLP[l])
                        hidden(u0, n0, c0, 0, 0)
                        hidden(u0 + 1, n0 + 1, c0 + 2, 2, 1)
                        first = 1
                    with dve.Fori(first, 4) as i:
                        for j in range(2):
                            split_low(u0 + 1 + j + 2 * i, (u0 + 1 + j) % 2)
                            hidden(u0 + j + 2 * i, n0 + j + 2 * i, c0 + 2 * j + 4 * i, 2 * j + 4 * i, j)
                    for f in range(NF):
                        last_phase = l == 1 and half == 1 and f == 1
                        if last_phase:
                            for q in range(3):
                                split_low(u0 + 13 + q, (u0 + 13 + q) % 2)
                            copy_result(0)
                        elif half == 1 and f == 1:
                            for q in range(4):
                                split_low(u0 + 13 + q, (u0 + 13 + q) % 2)
                                if q == 0:
                                    dve.wait_ge(x_ready, X_MLP[0] + 12)
                                    prep_x(H_K, h_high_buf, h_low_buf, C_KV, range(4))
                                    norm_sums(NORM_KV, range(1, 4))
                        else:
                            with dve.Fori(0, 2) as r:
                                for j in range(2):
                                    u = u0 + 8 + 4 * f + 1 + j
                                    split_low(u + 2 * r, u % 2)
                        for m in range(4):
                            if m < 3:
                                dve.wait_ge(out_done, OUT_MLP[l] + 6 * half + 3 * f + m + 1)
                            else:
                                dve.wait_ge(w_used, u0 + 8 + 4 * f + 4)
                            dve.tensor_tensor(xT[:, 4 * f + m, :], xT[:, 4 * f + m, :], O[m][:, :], ALU.add).then_inc(x_ready, 1)

            def copy_result(f):
                for i in (1, 3):
                    dve.wait_ge(y_turned, 4 * f + i + 1)
                    dve.tensor_copy(out_sb[:, i, f * S:(f + 1) * S], I[i][:, :]).then_inc(y_copied[1], 1)

            dve.memset(bias_rows[0:H, S:REL], MASKED).then_inc(bias_rows_ready, 1)
            dve.wait_ge(tok_rooted, 1)
            dve.reciprocal(tok_rstd[:, :], tok_root[:, :]).then_inc(tok_inverse, 1)
            dve.wait_ge(tok_inverse, 1)
            for i in range(TT):
                dve.tensor_scalar(h_tok[:, i, :], x_tok[:, i, :], tok_rstd[:, i:i + 1], None, ALU.mult).then_inc(h_tok_ready, 1)
            dve.wait_ge(xt_done, TT)
            for c in DVE_CHUNKS:
                dve.tensor_copy(xT[:, c, :], bank[c][:, :]).then_inc(x_ready, 1)
            split_low(0, 0)
            dve.wait_ge(params_ready, 1)
            for c in range(KC):
                dve.wait_ge(h_high, H_POOL + c + 1)
                input_low(m_low_buf[:, c, :], I[c % 4][:, :], params[:, C_MIX + c:C_MIX + c + 1], m_high_buf[:, c, :])
                if c == 4:
                    dve.wait_ge(lam_landed, 64)
                    for b in range(2):
                        dve.tensor_tensor_reduce(out=lam_junk, in0=lam_sb[:, 2 * b, :], in1=lam_sb[:, 2 * b + 1, :], scale=1.0,
                                                 scalar=0.0, op0=ALU.mult, op1=ALU.add, accum_out=lam_dots[:, b:b + 1]).then_inc(lam_dot, 1)
                        dve.wait_ge(lam_dot, b + 1)
            dve.wait_ge(first_low, 1)
            dve.memset(wait_cell[0:1, 0:1], 0.0).then_inc(w_low, 1)
            dve.tensor_scalar(qk_gain[:, :], params[:, C_QN:C_QN + 1], params[:, C_KN:C_KN + 1], HD ** -0.5, ALU.mult, ALU.mult)
            dve.tensor_scalar(sub_gain[:, :], params[:, C_SUB:C_SUB + 1], 1.0 - LAMBDA_INIT, None, ALU.mult).then_inc(params_ready, 1)
            dve.wait_ge(xt_copied, len(ACT_CHUNKS))
            for c in range(KC + 1):
                if c < KC:
                    if c < KC - 1:
                        dve.wait_ge(pool_done, c + 1)
                    else:
                        dve.wait_ge(w_used, 1)
                    dve.scalar_tensor_tensor(xT[:, c, :], O[c % 4][:, :], params[:, C_PSCALE + c:C_PSCALE + c + 1], xT[:, c, :],
                                             ALU.mult, ALU.add).then_inc(x_ready, 1)
                if c >= 1:
                    dve.wait_ge(x_ready, X_POOL + c)
                    dve.wait_ge(h_high, H_MLP[0] + c)
                    input_low(h_low_buf[:, c - 1, :], xT[:, c - 1, :], params[:, C_MLP + c - 1:C_MLP + c], h_high_buf[:, c - 1, :])
            dve.wait_ge(lam_exp, 1)
            dve.tensor_scalar(neg_lam[:, :], lam_exps[:, 1:2], lam_exps[:, 0:1], -LAMBDA_INIT, ALU.subtract, ALU.add).then_inc(lam_ready, 1)
            dve.wait_ge(bias_stored, 16)
            mlp(0)

            def take_k(n):
                dve.wait_ge(k_proj, n + 1)
                dve.tensor_tensor(kf, I[0][:, :], rstd_bc, ALU.mult).then_inc(kf_ready, 1)

            def take_q(n):
                dve.wait_ge(w_used, U_HEAD + 1 + 2 * n)
                dve.tensor_tensor(qf, I[1][:, :], rstd_bc, ALU.mult).then_inc(qf_ready, 1)

            def take_v(n):
                dve.wait_ge(w_used, U_HEAD + 2 + 2 * n)
                dve.tensor_tensor(vf, I[2][:, :], rstd_bc, ALU.mult).then_inc(vf_ready, 1)

            def kq_inverses(n):
                dve.wait_ge(kq_rooted, n + 1)
                dve.reciprocal(kq_rstd_buf[:, :], kq_root_buf[:, :]).then_inc(kq_inverse, 1)
                dve.wait_ge(kq_inverse, n + 1)
                for b, (dst, s) in enumerate(((ksq, k_spread), (qsq, q_spread))):
                    dve.tensor_copy(dst.rearrange("p (g d) -> p g d", d=HD),
                                    kq_rstd_buf[:, 8 * b:8 * b + 8].unsqueeze(2).to_broadcast([P, 8, HD])).then_inc(s, 1)

            def kq_norms(n):
                dve.wait_ge(k_turned, n + 1)
                dve.tensor_tensor(kf, kf, I[0][:, :], ALU.mult).then_inc(kn_ready, 1)
                dve.wait_ge(q_turned, n + 1)
                dve.tensor_tensor(qf, qf, I[1][:, :], ALU.mult).then_inc(qn_ready, 1)

            def kq_lows(n):
                dve.wait_ge(kq_high, 3 * n + 1)
                dve.tensor_tensor(k_lo, kf, f32(k_hi), ALU.subtract).then_inc(kq_low, 1)
                for c in range(2):
                    r = slice(c * HD, (c + 1) * HD)
                    dve.wait_ge(kq_high, 3 * n + 2 + c)
                    dve.scalar_tensor_tensor(q_lo[c][r, :], qf[r, :], qk_gain[r, 0:1], f32(q_hi[c][r, :]),
                                             ALU.mult, ALU.subtract).then_inc(kq_low, 1)

            def v_lows(n):
                dve.wait_ge(v_high, n + 1)
                dve.tensor_tensor(v_lo, I[2][:, :], f32(v_hi), ALU.subtract).then_inc(v_low, 1)

            def scores(h, i):
                if i >= 2:
                    dve.wait_ge(a_ready, 4 * h + i - 1)
                dve.wait_ge(s_done, 8 * h + 2 * i + 2)
                dve.memset(wait_cell[0:1, i:i + 1], 0.0)
                for c in range(2):
                    j = 2 * i + c
                    t = p1(i) if c == 0 else p2_ring[i % 2][:, 0:P * (i + 1)]
                    dve.tensor_tensor_reduce(out=t, in0=O[j % 4][:, 0:P * (i + 1)], in1=bias_tile[:, P * (3 - i):S],
                                             scale=1.0, scalar=MASKED, op0=ALU.add, op1=ALU.max,
                                             accum_out=row_max[:, j:j + 1]).then_inc(s_taken, 1)
                dve.wait_ge(s_taken, 8 * h + 2 * i + 2)
                dve.tensor_scalar(neg_max[:, 2 * i:2 * i + 2], row_max[:, 2 * i:2 * i + 2], -1.0, None, ALU.mult).then_inc(max_ready, 1)

            def combine(h, i):
                t2 = p2_ring[i % 2][:, 0:P * (i + 1)]
                dve.wait_ge(exp_done, 8 * h + 2 * i + 2)
                dve.reciprocal(row_inv[:, 2 * i:2 * i + 2], row_sum[:, 2 * i:2 * i + 2]).then_inc(inv_ready, 1)
                dve.wait_ge(inv_ready, 4 * h + i + 1)
                dve.tensor_scalar(t2, t2, row_inv[:, 2 * i + 1:2 * i + 2], neg_lam[:, 0:1], ALU.mult, ALU.mult).then_inc(second_scaled, 1)
                dve.wait_ge(second_scaled, 4 * h + i + 1)
                dve.scalar_tensor_tensor(p1(i), p1(i), row_inv[:, 2 * i:2 * i + 1], t2, ALU.mult, ALU.add).then_inc(a_ready, 1)

            def at_lows(h):
                for b in range(3):
                    dve.wait_ge(at_high, 3 * h + b + 1)
                    dve.tensor_tensor(a_low_buf[:, 12 + b, 0:AT_COLS[b]], O[b][:, 0:AT_COLS[b]],
                                      f32(a_high_buf[:, 12 + b, 0:AT_COLS[b]]), ALU.subtract).then_inc(at_low, 1)

            def o_inverses(m):
                dve.wait_ge(o_rooted, m + 1)
                dve.reciprocal(o_rstd_buf[:, :], o_root_buf[:, :].rearrange("p (i b) -> p i b", b=2)[:, :, 0]).then_inc(o_inverse, 1)
                dve.wait_ge(o_inverse, m + 1)
                dve.tensor_copy(osq.rearrange("p (i n) -> p i n", i=TT), o_rstd_buf[:, :].unsqueeze(2).to_broadcast([P, TT, P]))\
                   .then_inc(o_spread, 1)

            def o_norm(m, b):
                dve.wait_ge(o_turned, m + 1)
                dst = o_all[:, m, :] if isinstance(m, int) else o_all[:, bass.ds(m, 1), :]
                dve.tensor_tensor(dst, of, b[:, :], ALU.mult).then_inc(o_ready, 1)

            def o_low(k):
                dve.wait_ge(h_high, H_O + k + 1)
                input_low(w_o_low[:, k, :], o_all[:, k, :], sub_gain[:, 0:1], w_o_high[:, k, :])

            dve.wait_ge(x_ready, X_MLP[0] + 16)
            prep_x(H_K, h_high_buf, h_low_buf, C_KV, range(4, KC))
            norm_sums(NORM_KV, range(4, KC))
            prep_x(H_Q, a_high_buf, a_low_buf, C_MIX + KC, range(4))
            norm_invert(NORM_KV)
            prep_x(H_Q, a_high_buf, a_low_buf, C_MIX + KC, range(4, KC))
            split_low(U_HEAD + 1, 0, 1024)
            norm_keep(NORM_KV)
            take_k(0)
            take_q(0)
            kq_inverses(0)
            kq_norms(0)
            kq_lows(0)
            take_v(0)
            split_low(U_HEAD + 2, 1)
            dve.wait_ge(lam_ready, 1)

            def head(h, first):
                dve.wait_ge(t_landed, 16 * h + 16)
                scores(h, 0)
                scores(h, 1)
                combine(h, 0)
                v_lows(h)
                scores(h, 2)
                combine(h, 1)
                scores(h, 3)
                combine(h, 2)
                combine(h, 3)
                take_k(h + 1)
                split_low(U_HEAD + 3 + 2 * h, 0, 1024)
                take_q(h + 1)
                at_lows(h)
                kq_inverses(h + 1)
                if not first:
                    o_inverses(h - 1)
                    o_norm(h - 1, O[3])
                kq_norms(h + 1)
                kq_lows(h + 1)
                take_v(h + 1)
                split_low(U_HEAD + 4 + 2 * h, 1)

            head(0, True)
            with dve.Fori(1, H - 1) as h:
                head(h, False)
            last = H - 1
            dve.wait_ge(t_landed, 16 * last + 16)
            scores(last, 0)
            scores(last, 1)
            o_low(0)
            combine(last, 0)
            v_lows(last)
            scores(last, 2)
            combine(last, 1)
            o_low(1)
            scores(last, 3)
            combine(last, 2)
            o_low(2)
            combine(last, 3)
            o_low(3)
            split_low(U_WO + 1, 0)
            o_inverses(last - 1)
            o_low(4)
            at_lows(last)
            o_norm(last - 1, O[3])
            o_low(5)
            o_low(6)
            split_low(U_WO + 2, 1)
            o_inverses(last)
            o_norm(last, O[1])
            o_low(last)
            for f in range(NF):
                acc = I if f == 0 else O
                for m in range(4):
                    if m < 3:
                        dve.wait_ge(out_done, OUT_WO + 3 * f + m + 1)
                    else:
                        dve.wait_ge(w_used, U_WO + 2 * f + 2)
                    dve.tensor_tensor(xT[:, 4 * f + m, :], xT[:, 4 * f + m, :], acc[m][:, :], ALU.add).then_inc(x_ready, 1)
                if f == 0:
                    split_low(U_WO + 3, 0)
                    dve.wait_ge(x_ready, X_WO + 4)
                    prep_x(H_MLP[1], h_high_buf, h_low_buf, C_MLP + KC, range(4))
                    norm_sums(NORM_MLP[1], range(1, 4))
                    split_low(U_WO + 4, 1)
            dve.wait_ge(x_ready, X_MLP[1])
            prep_x(H_MLP[1], h_high_buf, h_low_buf, C_MLP + KC, range(4, KC))
            mlp(1)
            copy_result(1)

        @block.tensor
        def _(pe):
            def product(acc, w_hi, w_lo, m_hi, m_lo, start, stop):
                pe.matmul(acc, w_hi, m_hi, start=start, stop=False)
                pe.matmul(acc, w_hi, m_lo, start=False, stop=False)
                return pe.matmul(acc, w_lo, m_hi, start=False, stop=stop)

            def column(s, at):
                return w_high_buf[s][:, at:at + P], w_low_buf[s][:, at:at + P]

            def norm_stats(n):
                pe.wait_ge(norm_sum, 7 * (n + 1))
                for i in range(TT):
                    last = pe.matmul(O[3][:, 2 * i:2 * i + 2], ssum[:, i * P:(i + 1) * P], all_ones[:, :], start=True, stop=True)
                last.then_inc(norm_stat, 1)

            def norm_turn(n):
                pe.wait_ge(norm_spread, n + 1)
                for i in range(TT):
                    last = pe.transpose(O[2][:, i * P:(i + 1) * P], rexp[:, i * P:(i + 1) * P], ident[:, :])
                last.then_inc(norm_turned, 1)

            def in_unit(u, s, c, odd, h_base=None, hooks={}):
                pe.wait_ge(w_low, u + 1)
                for j in range(2):
                    acc = I[2 * odd + j]
                    cc = c + j
                    if not isinstance(cc, int) or cc >= 4:
                        pe.wait_ge(z_taken, cc - 3)
                    for kc in range(KC):
                        if h_base is not None and j == 0:
                            pe.wait_ge(h_low, h_base + kc + 1)
                        if (j, kc) in hooks:
                            hooks[j, kc]()
                        w_hi, w_lo = column(s, kc * 2 * P + j * P)
                        last = product(acc[:, :], w_hi, w_lo, h_high_buf[:, kc, :], h_low_buf[:, kc, :], kc == 0, kc == KC - 1)
                    last.then_inc(in_first if j == 0 else w_used, 1)

            def out_unit(u, s, q, n_units, acc, inputs, ready, x_wait):
                pe.wait_ge(w_low, u + 1)
                for kk in range(4):
                    k = 4 * q + kk
                    ready(k)
                    for m in range(4):
                        if k == 0:
                            x_wait(m)
                        w_hi, w_lo = column(s, kk * S + m * P)
                        last = product(acc[m][:, :], w_hi, w_lo, *inputs(k), k == 0, q == n_units - 1 and kk == 3)
                        if q == n_units - 1 and kk == 3 and m < 3:
                            last.then_inc(out_done, 1)
                last.then_inc(w_used, 1)

            def mlp(l):
                for half in range(2):
                    u0, c0 = U_MLP[l] + 16 * half, 32 * l + 16 * half
                    first = 0
                    if half == 0:
                        in_unit(u0, u0 % 2, c0, 0, h_base=H_MLP[l])
                        in_unit(u0 + 1, (u0 + 1) % 2, c0 + 2, 1,
                                hooks={(0, 4): lambda: norm_stats(NORM_MLP[l]), (1, 1): lambda: norm_turn(NORM_MLP[l])})
                        first = 1
                    with pe.Fori(first, 4) as i:
                        for j in range(2):
                            in_unit(u0 + j + 2 * i, (u0 + j) % 2, c0 + 2 * j + 4 * i, j)

                    def ready(k):
                        pe.wait_ge(a_low, c0 + k + 1)

                    def inputs(k):
                        return a_high_buf[:, k, :], a_low_buf[:, k, :]

                    for f in range(NF):
                        def x_wait(m):
                            pe.wait_ge(x_ready, X_MLP[l] + 8 * half + 4 * f + m + 1 - 4)

                        for q in range(4):
                            u = u0 + 8 + 4 * f + q
                            out_unit(u, u % 2, q, 4, O, inputs, ready, x_wait)
                            if l == 1 and half == 1 and f == 1 and q == 0:
                                turn_result(0)

            def turn_result(f):
                pe.wait_ge(x_ready, X_MLP[1] + 8 + 4 * f + 4)
                for i in range(TT):
                    if f:
                        pe.wait_ge(y_copied[i % 2], i // 2 + 1)
                    for m in range(4):
                        last = pe.transpose(I[i][:, m * P:(m + 1) * P], xT[:, 4 * f + m, i * P:(i + 1) * P], ident[:, :])
                    last.then_inc(y_turned, 1)

            pe.wait_ge(consts_ready, 1)
            for i in range(TT):
                pe.wait_ge(x_landed[i], 16)
                for c in range(KC):
                    last = pe.transpose(bank[c][:, i * P:(i + 1) * P], x_tok[:, i, c * P:(c + 1) * P], ident[:, :])
                last.then_inc(xt_done, 1)
            pe.wait_ge(params_landed, 16 * 7)
            pe.wait_ge(xt_copied, 1)
            pe.transpose(I[0][:, 0:N_PARAM], param_rows[0:N_PARAM, :], ident[0:N_PARAM, 0:N_PARAM]).then_inc(params_turned, 1)
            pe.wait_ge(bands_landed, 16)
            pe.wait_ge(params_ready, 1)
            pe.wait_ge(h_tok_ready, TT)
            for c in range(KC):
                if c >= 4:
                    pe.wait_ge(h_low, c - 3)
                pe.matmul(I[c % 4][:, :], a_high_buf[:, 0, 0:P], a_high_buf[:, 0, :], start=True, stop=False)
                for i in range(TT):
                    n = min(BAND, S - i * P)
                    last = pe.matmul(I[c % 4][:, i * P:i * P + n], h_tok[:, i, c * P:(c + 1) * P],
                                     band_sb[:, min(i, 1), c // (KC // G), 0:n], start=False, stop=i == TT - 1)
                last.then_inc(mix_done, 1)
                if c == 5:
                    pe.wait_ge(bias_in_landed, 32)
                    pe.wait_ge(xt_copied, len(ACT_CHUNKS))
                    pe.matmul(O[0][0:H, :], rel_sb[:, :], bucket_sb[0:NB, :], start=True, stop=True).then_inc(bias_done, 1)
            pe.wait_ge(w_low, 1)
            pe.wait_ge(bias_rows_ready, 2)
            for c in range(KC):
                g, d = c // (KC // G), c % (KC // G)
                if c < 4:
                    pe.wait_ge(x_ready, max(c, 1))
                else:
                    pe.wait_ge(x_ready, X_POOL + c - 3)
                pe.wait_ge(h_low, H_POOL + 2 * g + 2)
                for kc in range(GD // P):
                    w_hi, w_lo = column(0, (2 * g + kc) * GD + d * P)
                    last = product(O[c % 4][:, :], w_hi, w_lo, m_high_buf[:, 2 * g + kc, :], m_low_buf[:, 2 * g + kc, :],
                                   kc == 0, kc == GD // P - 1)
                last.then_inc(pool_done if c < KC - 1 else w_used, 1)
            mlp(0)

            def project(u, s, at, acc, hi, lo, done, chunks=range(KC), ready=None):
                for kc in chunks:
                    if ready is not None:
                        pe.wait_ge(h_low, ready + kc + 1)
                    w_hi, w_lo = column(s, at + kc * P)
                    last = product(acc[:, :], w_hi, w_lo, hi[:, kc, :], lo[:, kc, :], kc == 0, kc == KC - 1)
                if done is not None:
                    last.then_inc(done, 1)

            def kq_stats(n):
                pe.wait_ge(kq_sq, 2 * n + 2)
                for b, t in enumerate((ksq, qsq)):
                    for i in range(TT):
                        last = pe.matmul(I[3][:, 8 * b + 2 * i:8 * b + 2 * i + 2], t[:, i * P:(i + 1) * P], group_ones[:, :],
                                         start=True, stop=True)
                last.then_inc(kq_stat, 1)

            def o_stats(m, b):
                pe.wait_ge(o_copied, 2 * m + 2)
                for i in range(TT):
                    last = pe.matmul(b[:, 16 + 2 * i:18 + 2 * i], osq[:, i * P:(i + 1) * P], all_halves[:, :], start=True, stop=True)
                last.then_inc(o_stat, 1)

            def turn(src, b, ready, n, done):
                pe.wait_ge(ready, n + 1)
                for i in range(TT):
                    last = pe.transpose(b[:, i * P:(i + 1) * P], src[:, i * P:(i + 1) * P], ident[:, :])
                last.then_inc(done, 1)

            def scores(h, first):
                pe.wait_ge(kq_low, 3 * h + 3)
                if not first:
                    pe.wait_ge(at_low, 3 * h)
                for j in range(2 * TT):
                    i, c = j // 2, j % 2
                    if j == 3 and not first:
                        pe.wait_ge(o_copied, 2 * h)
                    if j >= 4:
                        pe.wait_ge(s_taken, 8 * h + j - 3)
                    n, q = P * (i + 1), slice(i * P, (i + 1) * P)
                    product(O[j % 4][:, 0:n], q_hi[c][:, q], q_lo[c][:, q], k_hi[:, 0:n], k_lo[:, 0:n], True, True).then_inc(s_done, 1)

            def turn_probs(h):
                pe.wait_ge(s_taken, 8 * h + 8)
                for i in range(TT):
                    pe.wait_ge(a_ready, 4 * h + i + 1)
                    for j in range(i + 1):
                        b, at = AT_PLACE[j]
                        at += (i - j) * P
                        last = pe.transpose(O[b][:, at:at + P], p1(i)[:, j * P:(j + 1) * P], ident[:, :])
                last.then_inc(at_done, 1)

            def values(h):
                pe.wait_ge(at_low, 3 * h + 3)
                for j in range(TT):
                    b, at = AT_PLACE[j]
                    n = S - j * P
                    last = product(O[3][:, j * P:S], v_hi[:, j * P:(j + 1) * P], v_lo[:, j * P:(j + 1) * P],
                                   a_high_buf[:, 12 + b, at:at + n], a_low_buf[:, 12 + b, at:at + n], j == 0, j == TT - 1)
                last.then_inc(pv_done, 1)

            pe.wait_ge(w_low, U_HEAD + 1)
            project(U_HEAD, 1, 0, I[0], h_high_buf, h_low_buf, k_proj, ready=H_K)
            norm_stats(NORM_KV)
            project(U_HEAD, 1, 1024, I[1], a_high_buf, a_low_buf, None, range(0, 6), ready=H_Q)
            norm_turn(NORM_KV)
            project(U_HEAD, 1, 1024, I[1], a_high_buf, a_low_buf, w_used, range(6, KC), ready=H_Q)
            pe.wait_ge(w_low, U_HEAD + 2)
            project(U_HEAD + 1, 0, 0, I[2], h_high_buf, h_low_buf, None, range(0, 4))
            kq_stats(0)
            project(U_HEAD + 1, 0, 0, I[2], h_high_buf, h_low_buf, None, range(4, 7))
            turn(ksq, I[0], k_spread, 0, k_turned)
            turn(qsq, I[1], q_spread, 0, q_turned)
            project(U_HEAD + 1, 0, 0, I[2], h_high_buf, h_low_buf, w_used, range(7, KC))
            turn(vf, I[2], vf_ready, 0, v_turned)
            pe.wait_ge(const_steps, CONST_STEPS + 4)

            def head(h, first):
                n = h + 1
                scores(h, first)
                pe.wait_ge(w_low, U_HEAD + 1 + 2 * n)
                project(None, 1, 0, I[0], h_high_buf, h_low_buf, k_proj)
                project(None, 1, 1024, I[1], a_high_buf, a_low_buf, w_used)
                turn_probs(h)
                pe.wait_ge(w_low, U_HEAD + 2 + 2 * n)
                pe.wait_ge(v_low, n)
                project(None, 0, 0, I[2], h_high_buf, h_low_buf, None, range(0, 1))
                if not first:
                    o_stats(h - 1, I[3])
                kq_stats(n)
                project(None, 0, 0, I[2], h_high_buf, h_low_buf, None, range(1, 4))
                turn(ksq, I[0], k_spread, n, k_turned)
                turn(qsq, I[1], q_spread, n, q_turned)
                if not first:
                    turn(osq, O[3], o_spread, h - 1, o_turned)
                project(None, 0, 0, I[2], h_high_buf, h_low_buf, w_used, range(4, KC))
                if not first:
                    pe.wait_ge(o_ready, h)
                values(h)
                turn(vf, I[2], vf_ready, n, v_turned)

            head(0, True)
            with pe.Fori(1, H - 1) as h:
                head(h, False)

            last_h = H - 1
            scores(last_h, False)
            o_stats(last_h - 1, I[3])
            pe.wait_ge(v_low, H)

            def wo_part(u, q, f, kks, banks=range(4)):
                acc = I if f == 0 else O
                for kk in kks:
                    k = 4 * q + kk
                    pe.wait_ge(h_low, H_O + k + 1)
                    for m in banks:
                        if k == 0 and f == 0 and m == 3:
                            pe.wait_ge(o_rooted, H - 1)
                        w_hi, w_lo = column(u % 2, kk * S + m * P)
                        last = product(acc[m][:, :], w_hi, w_lo, w_o_high[:, k, :], w_o_low[:, k, :], k == 0, k == KC - 1)
                        if k == KC - 1 and m < 3:
                            last.then_inc(out_done, 1)
                return last

            pe.wait_ge(w_low, U_WO + 1)
            wo_part(U_WO, 0, 0, range(4)).then_inc(w_used, 1)
            turn_probs(last_h)
            pe.wait_ge(w_low, U_WO + 2)
            wo_part(U_WO + 1, 1, 0, [0])
            turn(osq, O[3], o_spread, last_h - 1, o_turned)
            wo_part(U_WO + 1, 1, 0, [1])
            pe.wait_ge(o_ready, last_h)
            values(last_h)
            wo_part(U_WO + 1, 1, 0, [2])
            o_stats(last_h, O[0])
            pe.wait_ge(w_low, U_WO + 3)
            wo_part(U_WO + 2, 0, 1, range(0, 2), [2, 3])
            turn(osq, O[1], o_spread, last_h, o_turned)
            wo_part(U_WO + 2, 0, 1, range(2, 4), [2, 3])
            wo_part(U_WO + 1, 1, 0, [3]).then_inc(w_used, 1)
            wo_part(U_WO + 2, 0, 1, range(4), [0, 1]).then_inc(w_used, 1)
            pe.wait_ge(w_low, U_WO + 4)
            wo_part(U_WO + 3, 1, 1, range(4)).then_inc(w_used, 1)
            mlp(1)
            turn_result(1)


_INS = ["x", "norm_mix", "norm_mlp", "pool_w", "pool_scale", "kv_norm", "w_kv", "k_norm", "rel_bias", "w_q", "q_norm",
        "lam_q1", "lam_k1", "lam_q2", "lam_k2", "subln", "w_o", "w_mlp_in", "w_mlp_out"]


def kernel(**inputs):
    import concourse.bacc as bacc
    from concourse.bass_utils import run_bass_kernel_spmd

    nc = bacc.Bacc("TRN2", target_bir_lowering=False, num_devices=1)
    arrays = {name: np.ascontiguousarray(inputs[name]) for name in _INS}
    arrays["bucket_rows"] = distance_buckets()
    arrays["bands"] = pooling_bands()
    args = [nc.dram_tensor(f"in_{n}_dram", a.shape, mybir.dt.from_np(a.dtype), kind="ExternalInput").ap() for n, a in arrays.items()]
    out = nc.dram_tensor("out_0_dram", (1, S, D), mybir.dt.float32, kind="ExternalOutput").ap()
    build_program(nc, *args, out)
    r = run_bass_kernel_spmd(nc, [{f"in_{n}_dram": a for n, a in arrays.items()}], core_ids=[0])
    return r.results[0]["out_0_dram"]
```

```python
import math

import numpy as np

import concourse.bass as bass
from concourse import mybir
from contextlib import ExitStack

D = 1024
S = 512
P = 128
KC = D // P
TT = S // P
WINDOWS = (2, 4, 8, 16)
G = len(WINDOWS)
GD = D // G
H = 8
HD = D // (2 * H)
FF = 4 * D
NB = 32
MAXD = 128
EPS = 1e-6
LAMBDA_INIT = 0.8 - 0.6 * math.exp(-0.3)
MASKED = -3.0e38
REL = 640
BAND = P + max(WINDOWS) - 1

UNIT = 2048
U_POOL = 0
U_MLP = (1, 53)
U_HEAD = 33
U_WO = 49
UNITS = 85
NF = 2
HALF_CHUNKS = FF // P // 2

C_MIX, C_MLP, C_PSCALE, C_KV, C_QN, C_KN, C_SUB = 0, 16, 32, 40, 48, 49, 50
N_PARAM = 51


def distance_buckets():
    rel = np.arange(S - 1, -1, -1)
    exact = NB // 2
    nf = np.maximum(rel, 1).astype(np.float32)
    large = exact + (np.log(nf / np.float32(exact)) / np.float32(math.log(MAXD / exact)) * np.float32(NB - exact)).astype(np.int32)
    bucket = np.where(rel < exact, rel, np.minimum(large, NB - 1))
    return (np.arange(NB)[:, None] == bucket[None, :]).astype(np.float32)


def pooling_bands():
    bands = np.zeros((P, 2, G, BAND), np.float32)
    for g, w in enumerate(WINDOWS):
        for p in range(P):
            for n in range(p, min(p + w, BAND)):
                bands[p, 0, g, n] = np.float32(1) / np.float32(min(w, n + 1))
                bands[p, 1, g, n] = np.float32(1) / np.float32(w)
            bands[p, :, g, p] -= np.float32(1)
    return bands


def build_program(nc, x, norm_mix, norm_mlp, pool_w, pool_scale, kv_norm, w_kv, k_norm, rel_bias,
                  w_q, q_norm, lam_q1, lam_k1, lam_q2, lam_k2, subln, w_o, w_mlp_in, w_mlp_out,
                  bucket_rows, bands, out):
    F32, F32R = mybir.dt.float32, mybir.dt.float32r
    ALU, ACT = mybir.AluOpType, mybir.ActivationFunctionType
    ctx = ExitStack()
    with ctx:
        def sb(name, shape, dt=F32):
            return ctx.enter_context(nc.sbuf_tensor(name, shape, dt))

        def sem(name):
            return ctx.enter_context(nc.semaphore(name))

        xT = sb("xT", [P, KC, S])
        raw = [sb(f"raw{i}", [P, UNIT]) for i in range(2)]
        w_high_buf = [sb(f"w_high{i}", [P, UNIT], F32R) for i in range(2)]
        w_low_buf = [sb(f"w_low{i}", [P, UNIT], F32R) for i in range(2)]
        h_high_buf = sb("h_high_buf", [P, KC, S], F32R)
        h_low_buf = sb("h_low_buf", [P, KC, S], F32R)
        a_high_buf = sb("a_high_buf", [P, HALF_CHUNKS, S], F32R)
        a_low_buf = sb("a_low_buf", [P, HALF_CHUNKS, S], F32R)
        work = sb("work", [P, 11008])
        ident = sb("ident", [P, P])
        params = sb("params", [P, N_PARAM])
        all_ones = sb("all_ones", [P, 2])
        eps = sb("eps", [P, 1])
        qk_gain = sb("qk_gain", [P, 1])
        sub_gain = sb("sub_gain", [P, 1])
        rel_sb = sb("rel_sb", [NB, H])
        tok_ss = sb("tok_ss", [P, TT])
        tok_root = sb("tok_root", [P, TT])
        tok_rstd = sb("tok_rstd", [P, TT])
        norm_root = sb("norm_root", [P, 2 * TT])
        norm_rstd = sb("norm_rstd", [P, TT])
        lam_dots = sb("lam_dots", [P, 2])
        lam_exps = sb("lam_exps", [P, 2])
        neg_lam = sb("neg_lam", [P, 1])
        wait_cell = sb("wait_cell", [1, TT])
        pass_cell = sb("pass_cell", [1, 1])
        table_cell = sb("table_cell", [P, 1])
        row_max = sb("row_max", [P, 8])
        neg_max = sb("neg_max", [P, 8])
        row_sum = sb("row_sum", [P, 8])
        row_inv = sb("row_inv", [P, 8])
        kq_root_buf = sb("kq_root_buf", [P, 16])
        kq_rstd_buf = sb("kq_rstd_buf", [P, 16])
        kq_sum_buf = sb("kq_sum_buf", [P, 16])
        o_sum_buf = sb("o_sum_buf", [P, TT])
        o_root_buf = sb("o_root_buf", [P, TT])
        o_rstd_buf = sb("o_rstd_buf", [P, TT])

        def region(at, n):
            return work[:, at:at + n]

        kf, qf, vf = (region(i * S, S) for i in range(3))
        ksq, qsq, osq = (region((3 + i) * S, S) for i in range(3))
        of = region(3072, S)
        bias_tile = region(3584, S)
        p1_all = region(4096, 1280)
        p2_ring = [region(5376 + i * S, S) for i in range(2)]
        o_all = region(6400, H * S).rearrange("p (h t) -> p h t", h=H)
        rstd_bc = region(10496, S)
        relu_buf = [region(i * S, S) for i in range(2)]
        sq_buf = [region(1024 + i * S, S) for i in range(2)]
        ring = [region(2048 + i * S, S) for i in range(2)]
        ssum = region(3072, S)
        rexp = region(4096, S)
        out_sb = region(6400, TT * D).rearrange("p (i d) -> p i d", i=TT)
        x_tok = region(0, TT * D).rearrange("p (i d) -> p i d", i=TT)
        h_tok = region(4096, TT * D).rearrange("p (i d) -> p i d", i=TT)
        band_sb = region(8192, 2 * G * BAND).rearrange("p (f g n) -> p f g n", f=2, g=G)
        param_rows = region(9344, P)
        bucket_sb = region(9472, S)
        bias_rows = region(9984, REL)
        lam_sb = region(10624, 4 * HD).rearrange("p (v d) -> p v d", v=4)
        lam_junk = region(10880, HD)

        P1_AT = [0, 128, 384, 768]

        def p1(i):
            return p1_all[:, P1_AT[i]:P1_AT[i] + P * (i + 1)]

        m_high_buf, m_low_buf = a_high_buf[:, KC:2 * KC, :], a_low_buf[:, KC:2 * KC, :]
        ACT_CHUNKS, DVE_CHUNKS = (4, 5, 6, 7, 0), (1, 2, 3)

        k_hi, k_lo = a_high_buf[:, 8, :], a_low_buf[:, 8, :]
        q_hi, q_lo = [a_high_buf[:, 9 + c, :] for c in range(2)], [a_low_buf[:, 9 + c, :] for c in range(2)]
        v_hi, v_lo = a_high_buf[:, 11, :], a_low_buf[:, 11, :]
        w_o_high, w_o_low = a_high_buf[:, 0:KC, :], a_low_buf[:, 0:KC, :]
        AT_PLACE = [(0, 0), (1, 0), (2, 0), (1, 384)]
        AT_COLS = [512, 512, 256]

        bank = [ctx.enter_context(nc.psum_tensor(f"bank{i}", [P, S], F32)) for i in range(8)]
        O, I = bank[0:4], bank[4:8]

        scratch = nc.dram_tensor("bias_by_distance", (H, P, REL), F32, kind="Internal").ap()

        x_landed = [sem(f"x_landed{i}") for i in range(TT)]
        bands_landed = sem("bands_landed")
        params_landed = sem("params_landed")
        lam_landed = sem("lam_landed")
        bias_in_landed = sem("bias_in_landed")
        w_landed = [sem(f"w_landed{i}") for i in range(2)]
        bias_stored = sem("bias_stored")
        t_landed = sem("t_landed")
        out_stored = sem("out_stored")
        w_high = sem("w_high")
        w_low = sem("w_low")
        half_high = sem("half_high")
        half_low = sem("half_low")
        pool_low = sem("pool_low")
        w_used = sem("w_used")
        consts_ready = sem("consts_ready")
        zeros_ready = sem("zeros_ready")
        const_steps = sem("const_steps")
        params_turned = sem("params_turned")
        params_ready = sem("params_ready")
        bias_done = sem("bias_done")
        bias_rows_ready = sem("bias_rows_ready")
        tok_sq = sem("tok_sq")
        tok_rooted = sem("tok_rooted")
        tok_inverse = sem("tok_inverse")
        h_tok_ready = sem("h_tok_ready")
        h_tok_last = sem("h_tok_last")
        xt_done = sem("xt_done")
        xt_copied = sem("xt_copied")
        mix_done = sem("mix_done")
        pool_done = sem("pool_done")
        lam_dot = sem("lam_dot")
        lam_exp = sem("lam_exp")
        lam_ready = sem("lam_ready")
        x_ready = sem("x_ready")
        h_high = sem("h_high")
        h_low = sem("h_low")
        norm_sq = sem("norm_sq")
        norm_sum = sem("norm_sum")
        norm_stat = sem("norm_stat")
        norm_rooted = sem("norm_rooted")
        norm_inverse = sem("norm_inverse")
        norm_spread = sem("norm_spread")
        norm_turned = sem("norm_turned")
        rstd_ready = sem("rstd_ready")
        in_first = sem("in_first")
        z_taken = sem("z_taken")
        z_squared = sem("z_squared")
        a_high = sem("a_high")
        a_low = sem("a_low")
        out_done = sem("out_done")
        k_proj = sem("k_proj")
        kf_ready = sem("kf_ready")
        qf_ready = sem("qf_ready")
        vf_ready = sem("vf_ready")
        kq_raw_turned = sem("kq_raw_turned")
        kq_sq = sem("kq_sq")
        kq_sum = sem("kq_sum")
        kq_rooted = sem("kq_rooted")
        kq_inverse = sem("kq_inverse")
        k_spread = sem("k_spread")
        q_spread = sem("q_spread")
        k_turned = sem("k_turned")
        q_turned = sem("q_turned")
        kn_ready = sem("kn_ready")
        qn_ready = sem("qn_ready")
        kq_high = sem("kq_high")
        kq_low = sem("kq_low")
        v_turned = sem("v_turned")
        v_high = sem("v_high")
        v_low = sem("v_low")
        s_done = sem("s_done")
        s_taken = sem("s_taken")
        max_ready = sem("max_ready")
        table_in = sem("table_in")
        exp_done = sem("exp_done")
        inv_ready = sem("inv_ready")
        second_scaled = sem("second_scaled")
        a_ready = sem("a_ready")
        at_done = sem("at_done")
        at_high = sem("at_high")
        at_low = sem("at_low")
        pv_done = sem("pv_done")
        o_copied = sem("o_copied")
        o_raw_turned = sem("o_raw_turned")
        o_sq = sem("o_sq")
        o_sum = sem("o_sum")
        o_rooted = sem("o_rooted")
        o_inverse = sem("o_inverse")
        o_spread = sem("o_spread")
        o_turned = sem("o_turned")
        o_ready = sem("o_ready")
        y_turned = sem("y_turned")
        y_copied = [sem(f"y_copied{i}") for i in range(2)]
        y_added = sem("y_added")

        CONST_STEPS = 3
        X_POOL = len(DVE_CHUNKS)
        X_MLP, X_WO = (X_POOL + 8, X_POOL + 32), X_POOL + 24
        H_POOL, H_MLP, H_K, H_Q, H_O = 0, (8, 40), 16, 24, 32
        OUT_MLP, OUT_WO = (0, 18), 12
        NORM_MLP, NORM_KV = (0, 2), 1

        WARM_UP = 8
        POOL_UNITS = [1] + [U_HEAD + 2 + 2 * h for h in range(H)] + [U_WO + 1]

        def landed(u0, i=0):
            count = 16 * (u0 // 2 + 1)
            if u0 % 2 and u0 >= U_WO:
                count += 16 * H + 16
            return count + 16 * i

        def head_landed(n):
            return 16 * (U_HEAD // 2) + 32 * (n + 1)

        pool_v = pool_w[0].rearrange("g (k p) n -> p g k n", p=P)
        wk_v = w_kv.rearrange("(k p) n -> p k n", p=P)
        wq_v = w_q[0].rearrange("(k p) n -> p k n", p=P)
        wo_v = w_o[0].rearrange("(k p) n -> p k n", p=P)
        win_v = [w_mlp_in[l].rearrange("(k p) n -> p k n", p=P) for l in range(2)]
        wout_v = [w_mlp_out[l].rearrange("(k p) n -> p k n", p=P) for l in range(2)]

        def tile3(t, k):
            return t[:, :].rearrange("p (k n) -> p k n", k=k)

        block = ctx.enter_context(nc.Block())

        @block.sync
        def _(sp):
            for i in range(TT):
                sp.dma_start(x_tok[:, i, :], x[0, i * P:(i + 1) * P, :]).then_inc(x_landed[i], 16)
            sp.dma_start(band_sb, bands).then_inc(bands_landed, 16)
            sp.dma_start(param_rows[0:16, :], norm_mix.rearrange("l (k p) -> (l k) p", p=P)).then_inc(params_landed, 16)
            sp.dma_start(param_rows[16:32, :], norm_mlp.rearrange("l (k p) -> (l k) p", p=P)).then_inc(params_landed, 16)
            sp.dma_start(param_rows[32:40, :], pool_scale[0].rearrange("(k p) -> k p", p=P)).then_inc(params_landed, 16)
            sp.dma_start(param_rows[40:48, :], kv_norm.rearrange("(k p) -> k p", p=P)).then_inc(params_landed, 16)
            sp.dma_start(param_rows[48:49, :].rearrange("a (c d) -> a c d", c=2), q_norm[0:1, :].unsqueeze(1).to_broadcast([1, 2, HD]))\
              .then_inc(params_landed, 16)
            sp.dma_start(param_rows[49:50, :].rearrange("a (c d) -> a c d", c=2),
                         k_norm.rearrange("(a d) -> a d", a=1).unsqueeze(1).to_broadcast([1, 2, HD])).then_inc(params_landed, 16)
            sp.dma_start(param_rows[50:51, :], subln[0:1, :]).then_inc(params_landed, 16)
            sp.dma_start(raw[0][:, :].rearrange("p (g k n) -> p g k n", g=G, k=GD // P), pool_v).then_inc(w_landed[0], 16)

            sp.dma_start(tile3(raw[1], KC), win_v[0][:, :, 0:2 * P]).then_inc(w_landed[1], 16)
            sp.dma_start(bucket_sb[0:NB, :], bucket_rows).then_inc(bias_in_landed, 16)
            sp.dma_start(rel_sb[:, :], rel_bias).then_inc(bias_in_landed, 16)
            for v, lam in enumerate((lam_q1, lam_k1, lam_q2, lam_k2)):
                sp.dma_start(lam_sb[:, v, :], lam[0:1, :].to_broadcast([P, HD])).then_inc(lam_landed, 16)

            def slot_free(u):
                sp.wait_ge(w_low, u - 1)

            def load_in(l, u, s, column):
                slot_free(u)
                sp.dma_start(tile3(raw[s], KC), win_v[l][:, :, bass.ds(column, 2 * P)]).then_inc(w_landed[s], 16)

            def load_mlp(l):
                for half in range(2):
                    u0 = U_MLP[l] + 16 * half
                    if l == 0 and half == 0:
                        load_in(l, u0 + 1, 0, 2 * P)
                        first = 1
                    else:
                        first = 0
                    with sp.Fori(first, 4) as i:
                        for j in range(2):
                            load_in(l, u0 + 2 * i + j, (u0 + j) % 2, half * 2048 + 512 * i + 256 * j)
                    for f in range(NF):
                        with sp.Fori(0, 2) as r:
                            for j in range(2):
                                u = u0 + 8 + 4 * f + j
                                slot_free(u + 2 * r)
                                sp.dma_start(tile3(raw[u % 2], 4),
                                             wout_v[l][:, bass.ds(half * HALF_CHUNKS + 8 * r + 4 * j, 4), f * S:(f + 1) * S])\
                                  .then_inc(w_landed[u % 2], 16)

            load_mlp(0)
            with sp.Fori(0, H) as n:
                slot_free(U_HEAD + 2 * n)
                sp.dma_start(tile3(raw[1][:, 0:1024], KC), wk_v[:, :, bass.ds(n * P, P)]).then_inc(w_landed[1], 16)
                sp.dma_start(tile3(raw[1][:, 1024:2048], KC), wq_v[:, :, bass.ds(n * P, P)]).then_inc(w_landed[1], 16)
                slot_free(U_HEAD + 1 + 2 * n)
                sp.dma_start(tile3(raw[0][:, 0:1024], KC), wk_v[:, :, bass.ds(D + n * P, P)]).then_inc(w_landed[0], 16)
            for f in range(NF):
                for q in range(2):
                    u = U_WO + 2 * f + q
                    slot_free(u)
                    if u == U_WO:
                        for b in range(2):
                            sp.dma_start(tile3(raw[1][:, b * 1024:(b + 1) * 1024], 2),
                                         wo_v[:, 2 * b:2 * b + 2, 0:S]).then_inc(w_landed[1], 16)
                    else:
                        sp.dma_start(tile3(raw[u % 2], 4), wo_v[:, 4 * q:4 * q + 4, f * S:(f + 1) * S])\
                          .then_inc(w_landed[u % 2], 16)
            load_mlp(1)
            for f in range(NF):
                for i in range(TT):
                    sp.wait_ge(y_added, 4 * f + i + 1)
                    sp.dma_start(out[0, i * P:(i + 1) * P, f * S:(f + 1) * S], out_sb[:, i, f * S:(f + 1) * S])\
                      .then_inc(out_stored, 16)
            sp.wait_ge(out_stored, 16 * NF * TT)

        @block.gpsimd
        def _(pool):
            steps = [0]

            def done(instruction):
                steps[0] += 1
                instruction.then_inc(const_steps, 1)
                pool.wait_ge(const_steps, steps[0])

            pool.memset(a_high_buf[:, 0, :].bitcast(F32), 0.0).then_inc(zeros_ready, 1)
            done(pool.memset(ident[:, :], 0.0))
            done(pool.affine_select(out=ident[:, :], in_=ident[:, :], compare_op=ALU.not_equal, fill=1.0, base=0,
                                    pattern=[[-1, P]], channel_multiplier=1))
            done(pool.memset(all_ones[:, :], 1.0))
            pool.memset(eps[:, :], EPS).then_inc(consts_ready, 1)

            def split_low(u):
                pool.wait_ge(w_high, u + 1)
                pool.tensor_tensor(w_low_buf[u % 2][:, :], raw[u % 2][:, :], w_high_buf[u % 2][:, :].bitcast(F32), ALU.subtract)\
                    .then_inc(pool_low, 1)

            def split_low_halves(h, u):
                pool.wait_ge(half_high, h + 1)
                pool.tensor_tensor(w_low_buf[1][:, 0:UNIT // 2], raw[1][:, 0:UNIT // 2], w_high_buf[1][:, 0:UNIT // 2].bitcast(F32),
                                   ALU.subtract).then_inc(half_low, 1)
                pool.wait_ge(half_low, h + 1)
                pool.wait_ge(w_high, u + 1)
                pool.tensor_tensor(w_low_buf[1][:, UNIT // 2:], raw[1][:, UNIT // 2:], w_high_buf[1][:, UNIT // 2:].bitcast(F32),
                                   ALU.subtract).then_inc(pool_low, 1)

            split_low(POOL_UNITS[0])
            pool.wait_ge(bias_rows_ready, 2)
            pool.dma_start(scratch, bias_rows[0:H, :].unsqueeze(1).to_broadcast([H, P, REL])).then_inc(bias_stored, 16)
            pool.wait_ge(bias_stored, 16)
            pool.wait_ge(w_used, U_HEAD)
            for q in (q_hi, q_lo):
                done(pool.memset(q[0][HD:P, :].bitcast(F32), 0.0))
                done(pool.memset(q[1][0:HD, :].bitcast(F32), 0.0))
            for h in range(H):
                if h:
                    pool.wait_ge(s_taken, 8 * h)
                pool.dma_start(bias_tile, bass.AP(tensor=scratch.tensor, offset=h * P * REL + P - 1, ap=[[REL - 1, P], [1, S]]))\
                    .then_inc(t_landed, 16)
                split_low_halves(h, POOL_UNITS[1 + h])
            split_low(POOL_UNITS[1 + H])

        @block.scalar
        def _(act):
            def split_high(u, s, landed_count, cols=UNIT):
                act.wait_ge(w_landed[s], landed_count)
                if not isinstance(u, int) or u >= 2:
                    act.wait_ge(w_used, u - 1)
                act.activation(w_high_buf[s][:, 0:cols], raw[s][:, 0:cols], ACT.Copy).then_inc(w_high, 1)

            def split_high_first(u, landed_count):
                act.wait_ge(w_landed[1], landed_count)
                act.wait_ge(w_used, u - 1)
                act.activation(w_high_buf[1][:, 0:UNIT // 2], raw[1][:, 0:UNIT // 2], ACT.Copy).then_inc(half_high, 1)

            def split_high_rest():
                act.activation(w_high_buf[1][:, UNIT // 2:], raw[1][:, UNIT // 2:], ACT.Copy).then_inc(w_high, 1)

            def input_high(dst, src, gain):
                act.activation(dst, src, ACT.Copy, scale=gain).then_inc(h_high, 1)

            def norm_squares(n, chunks=range(KC)):
                for c in chunks:
                    if c >= 3:
                        act.wait_ge(norm_sum, 7 * n + c - 2)
                    act.activation(ssum if c == 0 else ring[(c - 1) % 2], xT[:, c, :], ACT.Square).then_inc(norm_sq, 1)

            def norm_root_step(n):
                act.wait_ge(norm_stat, n + 1)
                act.activation(norm_root[:, :], O[3][:, 0:2 * TT], ACT.Sqrt, scale=1.0 / D, bias=eps[:, 0:1])\
                   .then_inc(norm_rooted, 1)

            def prep_x(h_base, x_base, dst, gain, chunks=range(KC)):
                for c in chunks:
                    act.wait_ge(x_ready, x_base + c + 1)
                    input_high(dst[:, c, :], xT[:, c, :], params[:, gain + c:gain + c + 1])

            def hidden(c, k):
                for j in range(2):
                    cc, kk = c + j, k + j
                    s = j
                    act.wait_ge(z_taken, cc + 1)
                    if not isinstance(cc, int) or cc >= 2:
                        act.wait_ge(a_low, cc - 1)
                    act.activation(sq_buf[s], relu_buf[s], ACT.Square).then_inc(z_squared, 1)
                    act.wait_ge(z_squared, cc + 1)
                    act.activation(a_high_buf[:, bass.ds(kk, 1), :] if not isinstance(kk, int) else a_high_buf[:, kk, :],
                                   sq_buf[s], ACT.Copy).then_inc(a_high, 1)

            def mlp(l):
                for half in range(2):
                    u0, c0 = U_MLP[l] + 16 * half, 32 * l + 16 * half
                    first = 0
                    if half == 0:
                        split_high(u0 + 1, (u0 + 1) % 2, landed(u0 + 1))
                        norm_squares(NORM_MLP[l], range(0 if l == 0 else 4, KC))
                        split_high(u0 + 2, u0 % 2, landed(u0 + 2))
                        norm_root_step(NORM_MLP[l])
                        hidden(c0, 0)
                        hidden(c0 + 2, 2)
                        first = 1
                    with act.Fori(first, 4) as i:
                        for j in range(2):
                            split_high(u0 + 1 + j + 2 * i, (u0 + 1 + j) % 2, landed(u0 + 1 + j, i))
                            hidden(c0 + 2 * j + 4 * i, 2 * j + 4 * i)
                    for f in range(NF):
                        u = u0 + 8 + 4 * f + 1
                        if l == 1 and half == 1 and f == 0:
                            for q in range(4):
                                split_high(u + q, (u + q) % 2, landed(u + q))
                                if q in (1, 2):
                                    copy_residual(q - 1)
                        elif half == 1 and f == 1:
                            for q in range(3):
                                split_high(u + q, (u + q) % 2, landed(u + q))
                                if l == 0 and q == 0:
                                    prep_x(H_K, X_MLP[0] + 8, h_high_buf, C_KV, range(4))
                                    norm_squares(NORM_KV, range(4))
                            if l == 0:
                                split_high(U_HEAD, 1, head_landed(0))
                        else:
                            with act.Fori(0, 2) as r:
                                for j in range(2):
                                    split_high(u + j + 2 * r, (u + j) % 2, landed(u + j, r))

            act.wait_ge(consts_ready, 1)
            act.activation(tok_root[:, 0:1], eps[:, :], ACT.Sqrt).then_inc(tok_sq, 1)
            for i in range(TT):
                act.wait_ge(x_landed[i], 16)
                act.activation(h_tok[:, i, :], x_tok[:, i, :], ACT.Square, accum_out=tok_ss[:, i:i + 1]).then_inc(tok_sq, 1)
                if i >= TT - 2:
                    tiles = slice(0, TT - 1) if i == TT - 2 else slice(TT - 1, TT)
                    act.wait_ge(tok_sq, i + 2)
                    act.activation(tok_root[:, tiles], tok_ss[:, tiles], ACT.Sqrt, scale=1.0 / D, bias=eps[:, 0:1]).then_inc(tok_rooted, 1)
            act.wait_ge(xt_done, TT)
            for n, c in enumerate(ACT_CHUNKS):
                if n == 1:
                    act.wait_ge(tok_inverse, 2)
                    act.activation(h_tok[:, TT - 1, :], x_tok[:, TT - 1, :], ACT.Copy, scale=tok_rstd[:, TT - 1:TT]).then_inc(h_tok_last, 1)
                if n == 1:
                    act.wait_ge(params_turned, 1)
                    act.activation(params[:, :], I[0][:, 0:N_PARAM], ACT.Copy).then_inc(params_ready, 1)
                act.activation(xT[:, c, :], bank[c][:, :], ACT.Copy).then_inc(xt_copied, 1)
            act.wait_ge(params_ready, 1)
            for c in range(KC):
                act.wait_ge(mix_done, c + 1)
                input_high(m_high_buf[:, c, :], I[c % 4][:, :], params[:, C_MIX + c:C_MIX + c + 1])
                if c == 1:
                    split_high(0, 0, 16)
                if c == 4:
                    split_high(1, 1, 16)
                if c == 6:
                    act.wait_ge(bias_done, 1)
                    act.activation(bias_rows[0:H, 0:S], O[0][0:H, :], ACT.Copy).then_inc(bias_rows_ready, 1)
            act.wait_ge(lam_dot, 2)
            act.activation(lam_exps[:, :], lam_dots[:, :], ACT.Exp).then_inc(lam_exp, 1)
            prep_x(H_MLP[0], X_POOL, h_high_buf, C_MLP)
            mlp(0)

            def project(n):
                for b, dst in enumerate((ksq, qsq)):
                    act.wait_ge(kq_raw_turned, 2 * n + 1 + b)
                    act.activation(dst, I[b][:, :], ACT.Square).then_inc(kq_sq, 1)

            def kq_roots(n):
                act.wait_ge(kq_sum, 2 * n + 2)
                act.activation(kq_root_buf[:, :], kq_sum_buf[:, :], ACT.Sqrt, scale=1.0 / HD, bias=eps[:, 0:1]).then_inc(kq_rooted, 1)

            def kq_highs(n):
                act.wait_ge(kn_ready, n + 1)
                act.activation(k_hi, kf, ACT.Copy).then_inc(kq_high, 1)
                act.wait_ge(qn_ready, n + 1)
                for c in range(2):
                    r = slice(c * HD, (c + 1) * HD)
                    act.activation(q_hi[c][r, :], qf[r, :], ACT.Copy, scale=qk_gain[r, 0:1]).then_inc(kq_high, 1)

            def v_highs(n):
                act.wait_ge(v_turned, n + 1)
                act.activation(v_hi, I[2][:, :], ACT.Copy).then_inc(v_high, 1)

            def bring_table(f):
                act.activation(table_cell[:, :], eps[:, :], f).then_inc(table_in, 1)

            def exps(h, tiles=range(TT)):
                for i in tiles:
                    if i == 1:
                        v_highs(h)
                    act.wait_ge(max_ready, 4 * h + i + 1)
                    for c in range(2):
                        t = p1(i) if c == 0 else p2_ring[i % 2][:, 0:P * (i + 1)]
                        act.activation(t, t, ACT.Exp, bias=neg_max[:, 2 * i + c:2 * i + c + 1],
                                       accum_out=row_sum[:, 2 * i + c:2 * i + c + 1]).then_inc(exp_done, 1)

            def at_highs(h):
                act.wait_ge(at_done, h + 1)
                for b in range(3):
                    act.activation(a_high_buf[:, 12 + b, 0:AT_COLS[b]], O[b][:, 0:AT_COLS[b]], ACT.Copy).then_inc(at_high, 1)

            def o_squares(m, b):
                act.wait_ge(o_raw_turned, m + 1)
                act.activation(osq, b[:, :], ACT.Square).then_inc(o_sq, 1)

            def o_roots(m):
                act.wait_ge(o_sum, m + 1)
                act.activation(o_root_buf[:, :], o_sum_buf[:, :], ACT.Sqrt, scale=0.5 / HD, bias=eps[:, 0:1]).then_inc(o_rooted, 1)

            def o_copies(h):
                act.wait_ge(pv_done, h + 1)
                act.activation(of, O[3][:, :], ACT.Copy).then_inc(o_copied, 1)

            def o_high(k):
                act.wait_ge(o_ready, k + 1)
                input_high(w_o_high[:, k, :], o_all[:, k, :], sub_gain[:, 0:1])

            prep_x(H_K, X_MLP[0] + 8, h_high_buf, C_KV, range(4, KC))
            prep_x(H_Q, X_MLP[0] + 8, a_high_buf, C_MIX + KC, range(1))
            norm_squares(NORM_KV, range(4, 6))
            prep_x(H_Q, X_MLP[0] + 8, a_high_buf, C_MIX + KC, range(1, 2))
            norm_squares(NORM_KV, range(6, KC))
            prep_x(H_Q, X_MLP[0] + 8, a_high_buf, C_MIX + KC, range(2, 4))
            norm_root_step(NORM_KV)
            prep_x(H_Q, X_MLP[0] + 8, a_high_buf, C_MIX + KC, range(4, KC))
            split_high(U_HEAD + 1, 0, landed(U_HEAD + 1), 1024)
            project(0)
            split_high_first(U_HEAD + 2, head_landed(1))
            kq_roots(0)
            split_high_rest()
            bring_table(ACT.Exp)
            kq_highs(0)

            def head(h, first):
                exps(h)
                if not first:
                    o_squares(h - 1, I[3])
                split_high(U_HEAD + 3 + 2 * h, 0, landed(U_HEAD + 3, h), 1024)
                bring_table(ACT.Sqrt)
                split_high_first(U_HEAD + 4 + 2 * h, head_landed(h + 2))
                at_highs(h)
                project(h + 1)
                kq_roots(h + 1)
                if not first:
                    o_roots(h - 1)
                bring_table(ACT.Exp)
                kq_highs(h + 1)
                split_high_rest()
                o_copies(h)

            head(0, True)
            with act.Fori(1, H - 1) as h:
                head(h, False)
            act.wait_ge(w_used, U_WO - 1)
            o_high(0)
            for i in range(TT):
                exps(H - 1, [i])
                if i == 1:
                    o_squares(H - 2, I[3])
                    o_high(1)
                if 1 <= i < 3:
                    o_high(i + 1)
                if i == 1:
                    split_high(U_WO + 1, 0, landed(U_WO + 1))
            o_roots(H - 2)
            o_high(4)
            o_high(5)
            at_highs(H - 1)
            o_high(6)
            split_high(U_WO + 2, 1, landed(U_WO + 2))
            o_copies(H - 1)
            o_squares(H - 1, O[0])
            o_roots(H - 1)
            o_high(7)
            split_high(U_WO + 3, 0, landed(U_WO + 3))
            prep_x(H_MLP[1], X_WO, h_high_buf, C_MLP + KC, range(4))
            norm_squares(NORM_MLP[1], range(4))
            split_high(U_WO + 4, 1, landed(U_WO + 4))
            prep_x(H_MLP[1], X_WO, h_high_buf, C_MLP + KC, range(4, KC))

            def copy_residual(f):
                for i in (0, 2):
                    act.wait_ge(y_turned, 4 * f + i + 1)
                    act.activation(out_sb[:, i, f * S:(f + 1) * S], I[i][:, :], ACT.Copy).then_inc(y_copied[0], 1)

            mlp(1)

        @block.vector
        def _(dve):
            def f32(t):
                return t.bitcast(F32)

            def split_low(u, s, cols=UNIT):
                dve.wait_ge(w_high, u + 1)
                dve.tensor_tensor(w_low_buf[s][:, 0:cols], raw[s][:, 0:cols], f32(w_high_buf[s][:, 0:cols]), ALU.subtract)\
                   .then_inc(w_low, 1)

            def pass_low(n):
                dve.wait_ge(pool_low, n + 1)
                dve.memset(pass_cell[:, :], 0.0).then_inc(w_low, 1)

            def input_low(dst, src, gain, high):
                dve.scalar_tensor_tensor(dst, src, gain, f32(high), ALU.mult, ALU.subtract).then_inc(h_low, 1)

            def prep_x(h_base, hi, lo, gain, chunks=range(KC)):
                for c in chunks:
                    dve.wait_ge(h_high, h_base + c + 1)
                    input_low(lo[:, c, :], xT[:, c, :], params[:, gain + c:gain + c + 1], hi[:, c, :])

            def norm_sums(n, chunks=range(1, KC)):
                for c in chunks:
                    dve.wait_ge(norm_sq, 8 * n + c + 1)
                    if c > 1:
                        dve.wait_ge(norm_sum, 7 * n + c - 1)
                    dve.tensor_tensor(ssum, ssum, ring[(c - 1) % 2], ALU.add).then_inc(norm_sum, 1)

            def norm_invert(n):
                dve.wait_ge(norm_rooted, n + 1)
                dve.reciprocal(norm_rstd[:, :], norm_root[:, :].rearrange("p (i b) -> p i b", b=2)[:, :, 0]).then_inc(norm_inverse, 1)
                dve.wait_ge(norm_inverse, n + 1)
                dve.tensor_copy(rexp.rearrange("p (i n) -> p i n", i=TT), norm_rstd[:, :].unsqueeze(2).to_broadcast([P, TT, P]))\
                   .then_inc(norm_spread, 1)

            def norm_keep(n):
                dve.wait_ge(norm_turned, n + 1)
                dve.tensor_copy(rstd_bc, O[2][:, :]).then_inc(rstd_ready, 1)
                dve.wait_ge(rstd_ready, n + 1)

            def hidden(u, n_in, c, k, odd):
                for j in range(2):
                    cc, kk = c + j, k + j
                    if j == 0:
                        dve.wait_ge(in_first, n_in + 1)
                    else:
                        dve.wait_ge(w_used, u + 1)
                    if not isinstance(cc, int) or cc >= 2:
                        dve.wait_ge(z_squared, cc - 1)
                    dve.scalar_tensor_tensor(relu_buf[j], I[2 * odd + j][:, :], 0.0, rstd_bc, ALU.max, ALU.mult)\
                       .then_inc(z_taken, 1)
                    dve.wait_ge(a_high, cc + 1)
                    hi = a_high_buf[:, kk, :] if isinstance(kk, int) else a_high_buf[:, bass.ds(kk, 1), :]
                    lo = a_low_buf[:, kk, :] if isinstance(kk, int) else a_low_buf[:, bass.ds(kk, 1), :]
                    dve.tensor_tensor(lo, sq_buf[j], f32(hi), ALU.subtract).then_inc(a_low, 1)

            def mlp(l):
                for half in range(2):
                    u0, c0 = U_MLP[l] + 16 * half, 32 * l + 16 * half
                    n0 = 16 * l + 8 * half
                    first = 0
                    if half == 0:
                        split_low(u0 + 1, (u0 + 1) % 2)
                        norm_sums(NORM_MLP[l], range(1 if l == 0 else 4, KC))
                        split_low(u0 + 2, u0 % 2)
                        norm_invert(NORM_MLP[l])
                        norm_keep(NORM_MLP[l])
                        hidden(u0, n0, c0, 0, 0)
                        hidden(u0 + 1, n0 + 1, c0 + 2, 2, 1)
                        first = 1
                    with dve.Fori(first, 4) as i:
                        for j in range(2):
                            split_low(u0 + 1 + j + 2 * i, (u0 + 1 + j) % 2)
                            hidden(u0 + j + 2 * i, n0 + j + 2 * i, c0 + 2 * j + 4 * i, 2 * j + 4 * i, j)
                    for f in range(NF):
                        last_phase = l == 1 and half == 1 and f == 1
                        if last_phase:
                            for q in range(3):
                                split_low(u0 + 13 + q, (u0 + 13 + q) % 2)
                        elif l == 1 and half == 1:
                            for q in range(4):
                                split_low(u0 + 9 + q, (u0 + 9 + q) % 2)
                                if q in (1, 2):
                                    copy_residual(q - 1)
                        elif half == 1 and f == 1:
                            for q in range(4):
                                split_low(u0 + 13 + q, (u0 + 13 + q) % 2)
                                if q == 0:
                                    dve.wait_ge(x_ready, X_MLP[0] + 12)
                                    prep_x(H_K, h_high_buf, h_low_buf, C_KV, range(4))
                                    norm_sums(NORM_KV, range(1, 4))
                        else:
                            with dve.Fori(0, 2) as r:
                                for j in range(2):
                                    u = u0 + 8 + 4 * f + 1 + j
                                    split_low(u + 2 * r, u % 2)
                        for m in range(4):
                            if m < 3:
                                dve.wait_ge(out_done, OUT_MLP[l] + 6 * half + 3 * f + m + 1)
                            else:
                                dve.wait_ge(w_used, u0 + 8 + 4 * f + 4)
                            if l == 1 and half == 1:
                                if m % 2 == 0:
                                    dve.wait_ge(y_copied[0], 2 * f + m // 2 + 1)
                                y = out_sb[:, m, f * S:(f + 1) * S]
                                dve.tensor_tensor(y, y, O[m][:, :], ALU.add).then_inc(y_added, 1)
                            else:
                                dve.tensor_tensor(xT[:, 4 * f + m, :], xT[:, 4 * f + m, :], O[m][:, :], ALU.add).then_inc(x_ready, 1)

            def copy_residual(f):
                for i in (1, 3):
                    dve.wait_ge(y_turned, 4 * f + i + 1)
                    dve.tensor_copy(out_sb[:, i, f * S:(f + 1) * S], I[i][:, :]).then_inc(y_copied[1], 1)

            dve.memset(bias_rows[0:H, S:REL], MASKED).then_inc(bias_rows_ready, 1)
            dve.wait_ge(tok_rooted, 1)
            dve.reciprocal(tok_rstd[:, 0:TT - 1], tok_root[:, 0:TT - 1]).then_inc(tok_inverse, 1)
            dve.wait_ge(tok_inverse, 1)
            for i in range(TT - 1):
                if i == TT - 2:
                    dve.wait_ge(tok_rooted, 2)
                    dve.reciprocal(tok_rstd[:, TT - 1:TT], tok_root[:, TT - 1:TT]).then_inc(tok_inverse, 1)
                dve.tensor_scalar(h_tok[:, i, :], x_tok[:, i, :], tok_rstd[:, i:i + 1], None, ALU.mult).then_inc(h_tok_ready, 1)
            dve.wait_ge(xt_done, TT)
            for c in DVE_CHUNKS:
                dve.tensor_copy(xT[:, c, :], bank[c][:, :]).then_inc(x_ready, 1)
            dve.wait_ge(params_ready, 1)
            for c in range(KC):
                dve.wait_ge(h_high, H_POOL + c + 1)
                input_low(m_low_buf[:, c, :], I[c % 4][:, :], params[:, C_MIX + c:C_MIX + c + 1], m_high_buf[:, c, :])
                if c == 1:
                    split_low(0, 0)
                if c == 4:
                    dve.wait_ge(lam_landed, 64)
                    for b in range(2):
                        dve.tensor_tensor_reduce(out=lam_junk, in0=lam_sb[:, 2 * b, :], in1=lam_sb[:, 2 * b + 1, :], scale=1.0,
                                                 scalar=0.0, op0=ALU.mult, op1=ALU.add, accum_out=lam_dots[:, b:b + 1]).then_inc(lam_dot, 1)
                        dve.wait_ge(lam_dot, b + 1)
            pass_low(0)
            dve.tensor_scalar(qk_gain[:, :], params[:, C_QN:C_QN + 1], params[:, C_KN:C_KN + 1], HD ** -0.5, ALU.mult, ALU.mult)
            dve.tensor_scalar(sub_gain[:, :], params[:, C_SUB:C_SUB + 1], 1.0 - LAMBDA_INIT, None, ALU.mult).then_inc(params_ready, 1)
            dve.wait_ge(xt_copied, len(ACT_CHUNKS))
            for c in range(KC + 1):
                if c < KC:
                    if c < KC - 1:
                        dve.wait_ge(pool_done, c + 1)
                    else:
                        dve.wait_ge(w_used, 1)
                    dve.scalar_tensor_tensor(xT[:, c, :], O[c % 4][:, :], params[:, C_PSCALE + c:C_PSCALE + c + 1], xT[:, c, :],
                                             ALU.mult, ALU.add).then_inc(x_ready, 1)
                if c >= 1:
                    dve.wait_ge(x_ready, X_POOL + c)
                    dve.wait_ge(h_high, H_MLP[0] + c)
                    input_low(h_low_buf[:, c - 1, :], xT[:, c - 1, :], params[:, C_MLP + c - 1:C_MLP + c], h_high_buf[:, c - 1, :])
            dve.wait_ge(lam_exp, 1)
            dve.tensor_scalar(neg_lam[:, :], lam_exps[:, 1:2], lam_exps[:, 0:1], -LAMBDA_INIT, ALU.subtract, ALU.add).then_inc(lam_ready, 1)
            dve.wait_ge(bias_stored, 16)
            mlp(0)

            def take_k(n):
                dve.wait_ge(k_proj, n + 1)
                dve.tensor_tensor(kf, I[0][:, :], rstd_bc, ALU.mult).then_inc(kf_ready, 1)

            def take_q(n):
                dve.wait_ge(w_used, U_HEAD + 1 + 2 * n)
                dve.tensor_tensor(qf, I[1][:, :], rstd_bc, ALU.mult).then_inc(qf_ready, 1)

            def take_v(n):
                dve.wait_ge(w_used, U_HEAD + 2 + 2 * n)
                dve.tensor_tensor(vf, I[2][:, :], rstd_bc, ALU.mult).then_inc(vf_ready, 1)

            def kq_sums(n):
                for b, src in enumerate((ksq, qsq)):
                    dve.wait_ge(kq_sq, 2 * n + 1 + b)
                    dve.tensor_reduce(kq_sum_buf[:, 8 * b:8 * b + 8], src.rearrange("p (g d) -> p g d", d=HD), mybir.AxisListType.X, ALU.add)\
                       .then_inc(kq_sum, 1)

            def o_sums(m):
                dve.wait_ge(o_sq, m + 1)
                dve.tensor_reduce(o_sum_buf[:, :], osq.rearrange("p (i d) -> p i d", i=TT), mybir.AxisListType.X, ALU.add).then_inc(o_sum, 1)

            def kq_inverses(n):
                dve.wait_ge(kq_rooted, n + 1)
                dve.reciprocal(kq_rstd_buf[:, :], kq_root_buf[:, :]).then_inc(kq_inverse, 1)
                dve.wait_ge(kq_inverse, n + 1)
                for b, (dst, s) in enumerate(((ksq, k_spread), (qsq, q_spread))):
                    dve.tensor_copy(dst.rearrange("p (g d) -> p g d", d=HD),
                                    kq_rstd_buf[:, 8 * b:8 * b + 8].unsqueeze(2).to_broadcast([P, 8, HD])).then_inc(s, 1)

            def kq_norms(n):
                dve.wait_ge(k_turned, n + 1)
                dve.tensor_tensor(kf, kf, I[0][:, :], ALU.mult).then_inc(kn_ready, 1)
                dve.wait_ge(q_turned, n + 1)
                dve.tensor_tensor(qf, qf, I[1][:, :], ALU.mult).then_inc(qn_ready, 1)

            def kq_lows(n):
                dve.wait_ge(kq_high, 3 * n + 1)
                dve.tensor_tensor(k_lo, kf, f32(k_hi), ALU.subtract).then_inc(kq_low, 1)
                for c in range(2):
                    r = slice(c * HD, (c + 1) * HD)
                    dve.wait_ge(kq_high, 3 * n + 2 + c)
                    dve.scalar_tensor_tensor(q_lo[c][r, :], qf[r, :], qk_gain[r, 0:1], f32(q_hi[c][r, :]),
                                             ALU.mult, ALU.subtract).then_inc(kq_low, 1)

            def v_lows(n):
                dve.wait_ge(v_high, n + 1)
                dve.tensor_tensor(v_lo, I[2][:, :], f32(v_hi), ALU.subtract).then_inc(v_low, 1)

            def scores(h, i):
                if i >= 2:
                    dve.wait_ge(a_ready, 4 * h + i - 1)
                dve.wait_ge(s_done, 8 * h + 2 * i + 2)
                dve.memset(wait_cell[0:1, i:i + 1], 0.0)
                for c in range(2):
                    j = 2 * i + c
                    t = p1(i) if c == 0 else p2_ring[i % 2][:, 0:P * (i + 1)]
                    dve.tensor_tensor_reduce(out=t, in0=O[j % 4][:, 0:P * (i + 1)], in1=bias_tile[:, P * (3 - i):S],
                                             scale=1.0, scalar=MASKED, op0=ALU.add, op1=ALU.max,
                                             accum_out=row_max[:, j:j + 1]).then_inc(s_taken, 1)
                dve.wait_ge(s_taken, 8 * h + 2 * i + 2)
                dve.tensor_scalar(neg_max[:, 2 * i:2 * i + 2], row_max[:, 2 * i:2 * i + 2], -1.0, None, ALU.mult).then_inc(max_ready, 1)

            def combine(h, i):
                t2 = p2_ring[i % 2][:, 0:P * (i + 1)]
                dve.wait_ge(exp_done, 8 * h + 2 * i + 2)
                dve.reciprocal(row_inv[:, 2 * i:2 * i + 2], row_sum[:, 2 * i:2 * i + 2]).then_inc(inv_ready, 1)
                dve.wait_ge(inv_ready, 4 * h + i + 1)
                dve.tensor_scalar(t2, t2, row_inv[:, 2 * i + 1:2 * i + 2], neg_lam[:, 0:1], ALU.mult, ALU.mult).then_inc(second_scaled, 1)
                dve.wait_ge(second_scaled, 4 * h + i + 1)
                dve.scalar_tensor_tensor(p1(i), p1(i), row_inv[:, 2 * i:2 * i + 1], t2, ALU.mult, ALU.add).then_inc(a_ready, 1)

            def at_lows(h):
                for b in range(3):
                    dve.wait_ge(at_high, 3 * h + b + 1)
                    dve.tensor_tensor(a_low_buf[:, 12 + b, 0:AT_COLS[b]], O[b][:, 0:AT_COLS[b]],
                                      f32(a_high_buf[:, 12 + b, 0:AT_COLS[b]]), ALU.subtract).then_inc(at_low, 1)

            def o_inverses(m):
                dve.wait_ge(o_rooted, m + 1)
                dve.reciprocal(o_rstd_buf[:, :], o_root_buf[:, :]).then_inc(o_inverse, 1)
                dve.wait_ge(o_inverse, m + 1)
                dve.tensor_copy(osq.rearrange("p (i n) -> p i n", i=TT), o_rstd_buf[:, :].unsqueeze(2).to_broadcast([P, TT, P]))\
                   .then_inc(o_spread, 1)

            def o_norm(m, b):
                dve.wait_ge(o_turned, m + 1)
                dst = o_all[:, m, :] if isinstance(m, int) else o_all[:, bass.ds(m, 1), :]
                dve.tensor_tensor(dst, of, b[:, :], ALU.mult).then_inc(o_ready, 1)

            def o_low(k):
                dve.wait_ge(h_high, H_O + k + 1)
                input_low(w_o_low[:, k, :], o_all[:, k, :], sub_gain[:, 0:1], w_o_high[:, k, :])

            dve.wait_ge(x_ready, X_MLP[0] + 16)
            prep_x(H_K, h_high_buf, h_low_buf, C_KV, range(4, KC))
            prep_x(H_Q, a_high_buf, a_low_buf, C_MIX + KC, range(1))
            norm_sums(NORM_KV, range(4, 6))
            prep_x(H_Q, a_high_buf, a_low_buf, C_MIX + KC, range(1, 2))
            norm_sums(NORM_KV, range(6, KC))
            prep_x(H_Q, a_high_buf, a_low_buf, C_MIX + KC, range(2, 4))
            norm_invert(NORM_KV)
            prep_x(H_Q, a_high_buf, a_low_buf, C_MIX + KC, range(4, KC))
            split_low(U_HEAD + 1, 0, 1024)
            norm_keep(NORM_KV)
            take_k(0)
            take_q(0)
            kq_sums(0)
            kq_inverses(0)
            kq_norms(0)
            kq_lows(0)
            take_v(0)
            dve.wait_ge(lam_ready, 1)

            def head(h, first):
                dve.wait_ge(t_landed, 16 * h + 16)
                scores(h, 0)
                scores(h, 1)
                pass_low(h + 1)
                combine(h, 0)
                v_lows(h)
                scores(h, 2)
                combine(h, 1)
                scores(h, 3)
                combine(h, 2)
                combine(h, 3)
                take_k(h + 1)
                split_low(U_HEAD + 3 + 2 * h, 0, 1024)
                take_q(h + 1)
                if not first:
                    o_sums(h - 1)
                at_lows(h)
                kq_sums(h + 1)
                kq_inverses(h + 1)
                if not first:
                    o_inverses(h - 1)
                kq_norms(h + 1)
                if not first:
                    o_norm(h - 1, O[3])
                kq_lows(h + 1)
                take_v(h + 1)

            head(0, True)
            with dve.Fori(1, H - 1) as h:
                head(h, False)
            last = H - 1
            dve.wait_ge(t_landed, 16 * last + 16)
            scores(last, 0)
            scores(last, 1)
            pass_low(H)
            o_low(0)
            combine(last, 0)
            v_lows(last)
            scores(last, 2)
            o_low(1)
            combine(last, 1)
            scores(last, 3)
            o_low(2)
            combine(last, 2)
            combine(last, 3)
            o_low(3)
            pass_low(1 + H)
            o_sums(last - 1)
            o_inverses(last - 1)
            o_low(4)
            o_low(5)
            at_lows(last)
            o_norm(last - 1, O[3])
            o_low(6)
            split_low(U_WO + 2, 1)
            o_sums(last)
            o_inverses(last)
            o_norm(last, O[1])
            o_low(last)
            for f in range(NF):
                acc = I if f == 0 else O
                for m in range(4):
                    if m < 3:
                        dve.wait_ge(out_done, OUT_WO + 3 * f + m + 1)
                    else:
                        dve.wait_ge(w_used, U_WO + 2 * f + 2)
                    dve.tensor_tensor(xT[:, 4 * f + m, :], xT[:, 4 * f + m, :], acc[m][:, :], ALU.add).then_inc(x_ready, 1)
                if f == 0:
                    split_low(U_WO + 3, 0)
                    dve.wait_ge(x_ready, X_WO + 4)
                    prep_x(H_MLP[1], h_high_buf, h_low_buf, C_MLP + KC, range(4))
                    norm_sums(NORM_MLP[1], range(1, 4))
                    split_low(U_WO + 4, 1)
            dve.wait_ge(x_ready, X_MLP[1])
            prep_x(H_MLP[1], h_high_buf, h_low_buf, C_MLP + KC, range(4, KC))
            mlp(1)

        @block.tensor
        def _(pe):
            def product(acc, w_hi, w_lo, m_hi, m_lo, start, stop):
                pe.matmul(acc, w_hi, m_hi, start=start, stop=False)
                pe.matmul(acc, w_hi, m_lo, start=False, stop=False)
                return pe.matmul(acc, w_lo, m_hi, start=False, stop=stop)

            def column(s, at):
                return w_high_buf[s][:, at:at + P], w_low_buf[s][:, at:at + P]

            def norm_stats(n):
                pe.wait_ge(norm_sum, 7 * (n + 1))
                for i in range(TT):
                    last = pe.matmul(O[3][:, 2 * i:2 * i + 2], ssum[:, i * P:(i + 1) * P], all_ones[:, :], start=True, stop=True)
                last.then_inc(norm_stat, 1)

            def norm_turn(n):
                pe.wait_ge(norm_spread, n + 1)
                for i in range(TT):
                    last = pe.transpose(O[2][:, i * P:(i + 1) * P], rexp[:, i * P:(i + 1) * P], ident[:, :])
                last.then_inc(norm_turned, 1)

            def in_unit(u, s, c, odd, h_base=None, hooks={}):
                pe.wait_ge(w_low, u + 1)
                for j in range(2):
                    acc = I[2 * odd + j]
                    cc = c + j
                    if not isinstance(cc, int) or cc >= 4:
                        pe.wait_ge(z_taken, cc - 3)
                    for kc in range(KC):
                        if h_base is not None and j == 0:
                            pe.wait_ge(h_low, h_base + kc + 1)
                        if (j, kc) in hooks:
                            hooks[j, kc]()
                        w_hi, w_lo = column(s, kc * 2 * P + j * P)
                        last = product(acc[:, :], w_hi, w_lo, h_high_buf[:, kc, :], h_low_buf[:, kc, :], kc == 0, kc == KC - 1)
                    last.then_inc(in_first if j == 0 else w_used, 1)

            def out_unit(u, s, q, n_units, acc, inputs, ready, x_wait, by_token):
                pe.wait_ge(w_low, u + 1)
                for kk in range(4):
                    k = 4 * q + kk
                    ready(k)
                    for m in range(4):
                        if k == 0:
                            x_wait(m)
                        start, stop = k == 0, q == n_units - 1 and kk == 3
                        if by_token:
                            tile, w = slice(m * P, (m + 1) * P), slice(kk * S, (kk + 1) * S)
                            last = product(acc[m][:, :], a_high_buf[:, k, tile], a_low_buf[:, k, tile],
                                           w_high_buf[s][:, w], w_low_buf[s][:, w], start, stop)
                        else:
                            last = product(acc[m][:, :], *column(s, kk * S + m * P), *inputs(k), start, stop)
                        if q == n_units - 1 and kk == 3 and m < 3:
                            last.then_inc(out_done, 1)
                last.then_inc(w_used, 1)

            def mlp(l):
                for half in range(2):
                    u0, c0 = U_MLP[l] + 16 * half, 32 * l + 16 * half
                    first = 0
                    if half == 0:
                        in_unit(u0, u0 % 2, c0, 0, h_base=H_MLP[l])
                        in_unit(u0 + 1, (u0 + 1) % 2, c0 + 2, 1,
                                hooks={(0, 4): lambda: norm_stats(NORM_MLP[l]), (1, 1): lambda: norm_turn(NORM_MLP[l])})
                        first = 1
                    with pe.Fori(first, 4) as i:
                        for j in range(2):
                            in_unit(u0 + j + 2 * i, (u0 + j) % 2, c0 + 2 * j + 4 * i, j)

                    def ready(k):
                        pe.wait_ge(a_low, c0 + k + 1)

                    def inputs(k):
                        return a_high_buf[:, k, :], a_low_buf[:, k, :]

                    for f in range(NF):
                        def x_wait(m):
                            if l == 1 and half == 1 and f == 1:
                                pe.wait_ge(y_added, m + 1)
                            else:
                                pe.wait_ge(x_ready, X_MLP[l] + 8 * half + 4 * f + m + 1 - 4)

                        for q in range(4):
                            u = u0 + 8 + 4 * f + q
                            out_unit(u, u % 2, q, 4, O, inputs, ready, x_wait, l == 1 and half == 1)
                            if l == 1 and half == 1 and f == 0 and q < 2:
                                turn_stream(q)

            def turn_stream(f):
                pe.wait_ge(x_ready, X_MLP[1] + 8)
                pe.wait_ge(z_taken, 4 * HALF_CHUNKS)
                for i in range(TT):
                    if f:
                        pe.wait_ge(y_copied[i % 2], i // 2 + 1)
                    for m in range(4):
                        last = pe.transpose(I[i][:, m * P:(m + 1) * P], xT[:, 4 * f + m, i * P:(i + 1) * P], ident[:, :])
                    last.then_inc(y_turned, 1)

            pe.wait_ge(zeros_ready, 1)
            for _ in range(WARM_UP):
                pe.matmul(I[3][:, :], a_high_buf[:, 0, 0:P], a_high_buf[:, 0, :], start=True, stop=True)
            pe.wait_ge(consts_ready, 1)
            for i in range(TT):
                pe.wait_ge(x_landed[i], 16)
                for c in range(KC):
                    last = pe.transpose(bank[c][:, i * P:(i + 1) * P], x_tok[:, i, c * P:(c + 1) * P], ident[:, :])
                last.then_inc(xt_done, 1)
            pe.wait_ge(params_landed, 16 * 7)
            pe.wait_ge(xt_copied, 1)
            pe.transpose(I[0][:, 0:N_PARAM], param_rows[0:N_PARAM, :], ident[0:N_PARAM, 0:N_PARAM]).then_inc(params_turned, 1)
            pe.wait_ge(bands_landed, 16)
            pe.wait_ge(params_ready, 1)
            pe.wait_ge(h_tok_ready, TT - 1)
            pe.wait_ge(h_tok_last, 1)
            for c in range(KC):
                if c >= 4:
                    pe.wait_ge(h_low, c - 3)
                else:
                    pe.wait_ge(xt_copied, c + 1)
                pe.matmul(I[c % 4][:, :], a_high_buf[:, 0, 0:P], a_high_buf[:, 0, :], start=True, stop=False)
                for i in range(TT):
                    n = min(BAND, S - i * P)
                    last = pe.matmul(I[c % 4][:, i * P:i * P + n], h_tok[:, i, c * P:(c + 1) * P],
                                     band_sb[:, min(i, 1), c // (KC // G), 0:n], start=False, stop=i == TT - 1)
                last.then_inc(mix_done, 1)
                if c == 5:
                    pe.wait_ge(bias_in_landed, 32)
                    pe.wait_ge(xt_copied, len(ACT_CHUNKS))
                    pe.matmul(O[0][0:H, :], rel_sb[:, :], bucket_sb[0:NB, :], start=True, stop=True).then_inc(bias_done, 1)
            pe.wait_ge(w_low, 1)
            pe.wait_ge(bias_rows_ready, 2)
            for c in range(KC):
                g, d = c // (KC // G), c % (KC // G)
                if c < 4:
                    pe.wait_ge(x_ready, max(c, 1))
                else:
                    pe.wait_ge(x_ready, X_POOL + c - 3)
                pe.wait_ge(h_low, H_POOL + 2 * g + 2)
                for kc in range(GD // P):
                    w_hi, w_lo = column(0, (2 * g + kc) * GD + d * P)
                    last = product(O[c % 4][:, :], w_hi, w_lo, m_high_buf[:, 2 * g + kc, :], m_low_buf[:, 2 * g + kc, :],
                                   kc == 0, kc == GD // P - 1)
                last.then_inc(pool_done if c < KC - 1 else w_used, 1)
            mlp(0)

            def project(u, s, at, acc, hi, lo, done, chunks=range(KC), ready=None):
                for kc in chunks:
                    if ready is not None:
                        pe.wait_ge(h_low, ready + kc + 1)
                    w_hi, w_lo = column(s, at + kc * P)
                    last = product(acc[:, :], w_hi, w_lo, hi[:, kc, :], lo[:, kc, :], kc == 0, kc == KC - 1)
                if done is not None:
                    last.then_inc(done, 1)

            def turn_raw(n):
                turn(kf, I[0], kf_ready, n, kq_raw_turned)
                turn(qf, I[1], qf_ready, n, kq_raw_turned)

            def turn(src, b, ready, n, done):
                pe.wait_ge(ready, n + 1)
                for i in range(TT):
                    last = pe.transpose(b[:, i * P:(i + 1) * P], src[:, i * P:(i + 1) * P], ident[:, :])
                last.then_inc(done, 1)

            def scores(h, first):
                pe.wait_ge(kq_low, 3 * h + 3)
                if not first:
                    pe.wait_ge(at_low, 3 * h)
                for j in range(2 * TT):
                    i, c = j // 2, j % 2
                    if j == 3 and not first:
                        pe.wait_ge(o_copied, h)
                    if j == 4:
                        turn(vf, I[2], vf_ready, h, v_turned)
                        if not first:
                            turn(of, I[3], o_copied, h - 1, o_raw_turned)
                    if j >= 4:
                        pe.wait_ge(s_taken, 8 * h + j - 3)
                    n, q = P * (i + 1), slice(i * P, (i + 1) * P)
                    product(O[j % 4][:, 0:n], q_hi[c][:, q], q_lo[c][:, q], k_hi[:, 0:n], k_lo[:, 0:n], True, True).then_inc(s_done, 1)

            def turn_probs(h):
                pe.wait_ge(s_taken, 8 * h + 8)
                for i in range(TT):
                    pe.wait_ge(a_ready, 4 * h + i + 1)
                    for j in range(i + 1):
                        b, at = AT_PLACE[j]
                        at += (i - j) * P
                        last = pe.transpose(O[b][:, at:at + P], p1(i)[:, j * P:(j + 1) * P], ident[:, :])
                last.then_inc(at_done, 1)

            def values(h):
                pe.wait_ge(at_low, 3 * h + 3)
                for j in range(TT):
                    b, at = AT_PLACE[j]
                    n = S - j * P
                    last = product(O[3][:, j * P:S], v_hi[:, j * P:(j + 1) * P], v_lo[:, j * P:(j + 1) * P],
                                   a_high_buf[:, 12 + b, at:at + n], a_low_buf[:, 12 + b, at:at + n], j == 0, j == TT - 1)
                last.then_inc(pv_done, 1)

            pe.wait_ge(w_low, U_HEAD + 1)
            project(U_HEAD, 1, 0, I[0], h_high_buf, h_low_buf, k_proj, ready=H_K)
            project(U_HEAD, 1, 1024, I[1], a_high_buf, a_low_buf, None, range(0, 2), ready=H_Q)
            norm_stats(NORM_KV)
            project(U_HEAD, 1, 1024, I[1], a_high_buf, a_low_buf, None, range(2, 6), ready=H_Q)
            norm_turn(NORM_KV)
            project(U_HEAD, 1, 1024, I[1], a_high_buf, a_low_buf, w_used, range(6, KC), ready=H_Q)
            pe.wait_ge(w_low, U_HEAD + 2)
            project(U_HEAD + 1, 0, 0, I[2], h_high_buf, h_low_buf, None, range(0, 4))
            turn_raw(0)
            project(U_HEAD + 1, 0, 0, I[2], h_high_buf, h_low_buf, None, range(4, 7))
            turn(ksq, I[0], k_spread, 0, k_turned)
            turn(qsq, I[1], q_spread, 0, q_turned)
            project(U_HEAD + 1, 0, 0, I[2], h_high_buf, h_low_buf, w_used, range(7, KC))
            pe.wait_ge(half_low, 1)
            pe.wait_ge(kn_ready, 1)
            project(None, 1, 0, I[0], h_high_buf, h_low_buf, None, range(0, 4))
            pe.wait_ge(const_steps, CONST_STEPS + 4)

            def head(h, first):
                n = h + 1
                scores(h, first)
                pe.wait_ge(w_low, U_HEAD + 1 + 2 * n)
                project(None, 1, 0, I[0], h_high_buf, h_low_buf, k_proj, range(4 if first else 0, KC))
                project(None, 1, 1024, I[1], a_high_buf, a_low_buf, w_used)
                turn_probs(h)
                turn_raw(n)
                pe.wait_ge(w_low, U_HEAD + 2 + 2 * n)
                pe.wait_ge(v_low, n)
                project(None, 0, 0, I[2], h_high_buf, h_low_buf, None, range(0, 6))
                turn(ksq, I[0], k_spread, n, k_turned)
                turn(qsq, I[1], q_spread, n, q_turned)
                if not first:
                    turn(osq, O[3], o_spread, h - 1, o_turned)
                project(None, 0, 0, I[2], h_high_buf, h_low_buf, w_used, range(6, KC))
                if not first:
                    pe.wait_ge(o_ready, h)
                values(h)

            head(0, True)
            with pe.Fori(1, H - 1) as h:
                head(h, False)

            last_h = H - 1
            scores(last_h, False)
            def wo_part(u, q, f, kks, banks=range(4)):
                acc = I if f == 0 else O
                for kk in kks:
                    k = 4 * q + kk
                    pe.wait_ge(h_low, H_O + k + 1)
                    for m in banks:
                        if k == 0 and f == 0 and m == 2:
                            pe.wait_ge(v_low, H)
                        if k == 0 and f == 0 and m == 3:
                            pe.wait_ge(o_sq, H - 1)
                        w_hi, w_lo = column(u % 2, kk * S + m * P)
                        last = product(acc[m][:, :], w_hi, w_lo, w_o_high[:, k, :], w_o_low[:, k, :], k == 0, k == KC - 1)
                        if k == KC - 1 and m < 3:
                            last.then_inc(out_done, 1)
                return last

            pe.wait_ge(w_low, U_WO + 1)
            wo_part(U_WO, 0, 0, range(4)).then_inc(w_used, 1)
            turn_probs(last_h)
            pe.wait_ge(w_low, U_WO + 2)
            wo_part(U_WO + 1, 1, 0, [0])
            turn(osq, O[3], o_spread, last_h - 1, o_turned)
            wo_part(U_WO + 1, 1, 0, [1])
            pe.wait_ge(o_ready, last_h)
            values(last_h)
            wo_part(U_WO + 1, 1, 0, [2])
            turn(of, O[0], o_copied, last_h, o_raw_turned)
            pe.wait_ge(w_low, U_WO + 3)
            wo_part(U_WO + 2, 0, 1, range(0, 2), [2, 3])
            turn(osq, O[1], o_spread, last_h, o_turned)
            wo_part(U_WO + 2, 0, 1, range(2, 4), [2, 3])
            wo_part(U_WO + 1, 1, 0, [3]).then_inc(w_used, 1)
            wo_part(U_WO + 2, 0, 1, range(4), [0, 1]).then_inc(w_used, 1)
            pe.wait_ge(w_low, U_WO + 4)
            wo_part(U_WO + 3, 1, 1, range(4)).then_inc(w_used, 1)
            mlp(1)


_INS = ["x", "norm_mix", "norm_mlp", "pool_w", "pool_scale", "kv_norm", "w_kv", "k_norm", "rel_bias", "w_q", "q_norm",
        "lam_q1", "lam_k1", "lam_q2", "lam_k2", "subln", "w_o", "w_mlp_in", "w_mlp_out"]


def kernel(**inputs):
    import concourse.bacc as bacc
    from concourse.bass_utils import run_bass_kernel_spmd

    nc = bacc.Bacc("TRN2", target_bir_lowering=False, num_devices=1)
    arrays = {name: np.ascontiguousarray(inputs[name]) for name in _INS}
    arrays["bucket_rows"] = distance_buckets()
    arrays["bands"] = pooling_bands()
    args = [nc.dram_tensor(f"in_{n}_dram", a.shape, mybir.dt.from_np(a.dtype), kind="ExternalInput").ap() for n, a in arrays.items()]
    out = nc.dram_tensor("out_0_dram", (1, S, D), mybir.dt.float32, kind="ExternalOutput").ap()
    build_program(nc, *args, out)
    r = run_bass_kernel_spmd(nc, [{f"in_{n}_dram": a for n, a in arrays.items()}], core_ids=[0])
    return r.results[0]["out_0_dram"]
```
